# Optimizing a Trainium2 kernel written in Bass

```python
import math
import jax, jax.numpy as jnp
from jax import lax
import numpy as np

D_MODEL = 1024
BATCH = 1
SEQ = 512
DEPTH = 1
DEC_BATCH = 8
DEC_SEQ = 4
PAST_LEN = 4096
PAGE_SIZE = 128

MIX_DIM = D_MODEL
CONV_DIM = MIX_DIM // 2
CONV_HEADS = 8
CONV_WIDTH = 3
SSM_DIM = MIX_DIM - CONV_DIM
SSM_GROUP = 16
SSM_GROUPS = SSM_DIM // SSM_GROUP
SSM_STATE = 64
IN_DIM = 3 * CONV_DIM + SSM_DIM
N_EXPERT_GROUPS = 4
EXPERTS_PER_GROUP = 8
N_EXPERTS = N_EXPERT_GROUPS * EXPERTS_PER_GROUP
TOP_K = 2
D_EXPERT = D_MODEL // 4
N_MOD = 6
EPS = 1e-6
DT_MIN = 1e-3
DT_MAX = 1e-1

kernel_name = 'hymba_conv_s5_hmoe_adaln_step'

def _rmsnorm(x, g):
    xf = x.astype(jnp.float32)
    y = xf * lax.rsqrt(jnp.mean(xf * xf, axis=-1, keepdims=True) + EPS)
    return (y * g.astype(jnp.float32)).astype(x.dtype)

def _short_conv(v, buf, conv_w):
    s = v.shape[1]
    ext = jnp.concatenate([buf.astype(v.dtype), v], axis=1)
    out = ext[:, 0:s] * conv_w[0]
    for k in range(1, CONV_WIDTH):
        out = out + ext[:, k:k + s] * conv_w[k]
    return out, ext[:, s:]

def _complex_affine_combine(e1, e2):
    a1r, a1i, b1r, b1i = e1
    a2r, a2i, b2r, b2i = e2
    ar = a2r * a1r - a2i * a1i
    ai = a2r * a1i + a2i * a1r
    br = a2r * b1r - a2i * b1i + b2r
    bi = a2r * b1i + a2i * b1r + b2i
    return ar, ai, br, bi

def _s5(u, h0_re, h0_im, lambda_re, lambda_im, log_dt, b_re, b_im, c_re, c_im, d_skip, w_glu, b_glu):
    f32 = jnp.float32
    bsz, s, _ = u.shape
    uf = u.astype(f32)
    ug = uf.reshape(bsz, s, SSM_GROUPS, SSM_GROUP)
    lr = lambda_re.astype(f32)
    li = lambda_im.astype(f32)
    dt = jnp.exp(log_dt.astype(f32))[:, None]
    mag = jnp.exp(lr * dt)
    ar = mag * jnp.cos(li * dt)
    ai = mag * jnp.sin(li * dt)
    den = lr * lr + li * li
    fr = ((ar - 1.0) * lr + ai * li) / den
    fi = (ai * lr - (ar - 1.0) * li) / den
    br = b_re.astype(f32)
    bi = b_im.astype(f32)
    bbar_re = fr[..., None] * br - fi[..., None] * bi
    bbar_im = fr[..., None] * bi + fi[..., None] * br
    bu_re = jnp.einsum('bsgh,gph->bsgp', ug, bbar_re)
    bu_im = jnp.einsum('bsgh,gph->bsgp', ug, bbar_im)
    h0r = h0_re.astype(f32)
    h0i = h0_im.astype(f32)
    bu_re = bu_re.at[:, 0].add(ar * h0r - ai * h0i)
    bu_im = bu_im.at[:, 0].add(ar * h0i + ai * h0r)
    a_re = jnp.broadcast_to(ar, bu_re.shape)
    a_im = jnp.broadcast_to(ai, bu_im.shape)
    _, _, xr, xi = lax.associative_scan(_complex_affine_combine, (a_re, a_im, bu_re, bu_im), axis=1)
    y = (jnp.einsum('bsgp,ghp->bsgh', xr, c_re.astype(f32))
         - jnp.einsum('bsgp,ghp->bsgh', xi, c_im.astype(f32)))
    y = y.reshape(bsz, s, SSM_DIM) + d_skip.astype(f32) * uf
    g = jax.nn.gelu(y)
    out = g * jax.nn.sigmoid(g @ w_glu.astype(f32) + b_glu.astype(f32))
    return out.astype(u.dtype), xr[:, -1].astype(h0_re.dtype), xi[:, -1].astype(h0_im.dtype)

def _moe(h, w_rg, b_rg, w_re, b_re, w_gate, w_up, w_down):
    f32 = jnp.float32
    shp = h.shape
    t = h.reshape(-1, shp[-1])
    p_group = jax.nn.softmax((t @ w_rg + b_rg).astype(f32), axis=-1)
    g_idx = jnp.argmax(p_group, axis=-1)
    g_prob = jnp.max(p_group, axis=-1)
    g_onehot = jax.nn.one_hot(g_idx, N_EXPERT_GROUPS, dtype=f32)
    le = (jnp.einsum('td,gde->tge', t, w_re) + b_re).astype(f32)
    le_sel = jnp.einsum('tge,tg->te', le, g_onehot)
    top_v, top_i = lax.top_k(le_sel, TOP_K)
    w_k = jax.nn.softmax(top_v, axis=-1) * g_prob[:, None]
    e_idx = g_idx[:, None] * EXPERTS_PER_GROUP + top_i
    combine = jnp.einsum('tk,tke->te', w_k, jax.nn.one_hot(e_idx, N_EXPERTS, dtype=f32))
    out = jnp.zeros(t.shape, f32)
    for e in range(N_EXPERTS):
        he = jax.nn.silu(t @ w_gate[e]) * (t @ w_up[e])
        out = out + combine[:, e:e + 1] * (he @ w_down[e]).astype(f32)
    return out.astype(h.dtype).reshape(shp)

def _layer(x, c, conv_buf, s_re, s_im, w_ada, b_ada, norm1_g, norm2_g, w_in, conv_w,
           lambda_re, lambda_im, log_dt, ssm_b_re, ssm_b_im, ssm_c_re, ssm_c_im, ssm_d,
           w_glu, b_glu, out_norm_conv_g, out_norm_ssm_g, w_out, w_router_group,
           b_router_group, w_router_expert, b_router_expert, w_expert_gate, w_expert_up,
           w_expert_down):
    mod = jax.nn.silu(c) @ w_ada + b_ada
    sh1, sc1, gt1, sh2, sc2, gt2 = jnp.split(mod[:, None, :], N_MOD, axis=-1)
    h = _rmsnorm(x, norm1_g) * (1 + sc1) + sh1
    z = h @ w_in
    gate_b, gate_c, v_in, u = jnp.split(z, [CONV_DIM, 2 * CONV_DIM, 3 * CONV_DIM], axis=-1)
    conv_out, new_buf = _short_conv(gate_c * v_in, conv_buf, conv_w)
    y_conv = gate_b * conv_out
    y_ssm, new_re, new_im = _s5(u, s_re, s_im, lambda_re, lambda_im, log_dt, ssm_b_re, ssm_b_im,
                                ssm_c_re, ssm_c_im, ssm_d, w_glu, b_glu)
    merged = jnp.concatenate([_rmsnorm(y_conv, out_norm_conv_g), _rmsnorm(y_ssm, out_norm_ssm_g)], axis=-1)
    x = x + gt1 * (merged @ w_out)
    h = _rmsnorm(x, norm2_g) * (1 + sc2) + sh2
    x = x + gt2 * _moe(h, w_router_group, b_router_group, w_router_expert, b_router_expert,
                       w_expert_gate, w_expert_up, w_expert_down)
    return x, new_buf, new_re, new_im

def setup_inputs(seed: int = 0) -> dict:
    key = jax.random.key(seed)
    ks = jax.random.split(key, 40)
    f32 = jnp.float32

    def nrm(k, shape, scale):
        return jax.random.normal(k, shape, f32) * scale

    n_idx = jnp.arange(SSM_STATE, dtype=f32)
    log_dt = jax.random.uniform(ks[15], (DEPTH, SSM_GROUPS), f32, math.log(DT_MIN), math.log(DT_MAX))
    return {
        'x_prompt': nrm(ks[0], (BATCH, SEQ, D_MODEL), 1.0),
        'x_sample': nrm(ks[1], (DEC_BATCH, DEC_SEQ, D_MODEL), 1.0),
        'state_conv': nrm(ks[2], (DEPTH, DEC_BATCH, CONV_WIDTH - 1, CONV_DIM), 1.0),
        'state_ssm_re': nrm(ks[3], (DEPTH, DEC_BATCH, SSM_GROUPS, SSM_STATE), 0.1),
        'state_ssm_im': nrm(ks[4], (DEPTH, DEC_BATCH, SSM_GROUPS, SSM_STATE), 0.1),
        'c_prompt': nrm(ks[5], (BATCH, D_MODEL), 1.0),
        'c_sample': nrm(ks[6], (DEC_BATCH, D_MODEL), 1.0),
        'w_ada': nrm(ks[7], (DEPTH, D_MODEL, N_MOD * D_MODEL), 0.5 * D_MODEL ** -0.5),
        'b_ada': nrm(ks[8], (DEPTH, N_MOD * D_MODEL), 0.01),
        'norm1_g': 1.0 + nrm(ks[9], (DEPTH, D_MODEL), 0.01),
        'norm2_g': 1.0 + nrm(ks[10], (DEPTH, D_MODEL), 0.01),
        'w_in': nrm(ks[11], (DEPTH, D_MODEL, IN_DIM), D_MODEL ** -0.5),
        'conv_w': nrm(ks[12], (DEPTH, CONV_WIDTH, CONV_DIM), CONV_WIDTH ** -0.5),
        'lambda_re': -0.5 + nrm(ks[13], (DEPTH, SSM_GROUPS, SSM_STATE), 0.01),
        'lambda_im': math.pi * n_idx + nrm(ks[14], (DEPTH, SSM_GROUPS, SSM_STATE), 0.01),
        'log_dt': log_dt,
        'ssm_b_re': nrm(ks[16], (DEPTH, SSM_GROUPS, SSM_STATE, SSM_GROUP), (2 * SSM_GROUP) ** -0.5),
        'ssm_b_im': nrm(ks[17], (DEPTH, SSM_GROUPS, SSM_STATE, SSM_GROUP), (2 * SSM_GROUP) ** -0.5),
        'ssm_c_re': nrm(ks[18], (DEPTH, SSM_GROUPS, SSM_GROUP, SSM_STATE), SSM_STATE ** -0.5),
        'ssm_c_im': nrm(ks[19], (DEPTH, SSM_GROUPS, SSM_GROUP, SSM_STATE), SSM_STATE ** -0.5),
        'ssm_d': nrm(ks[20], (DEPTH, SSM_DIM), 1.0),
        'w_glu': nrm(ks[21], (DEPTH, SSM_DIM, SSM_DIM), SSM_DIM ** -0.5),
        'b_glu': nrm(ks[22], (DEPTH, SSM_DIM), 0.01),
        'out_norm_conv_g': 1.0 + nrm(ks[23], (DEPTH, CONV_DIM), 0.01),
        'out_norm_ssm_g': 1.0 + nrm(ks[24], (DEPTH, SSM_DIM), 0.01),
        'w_out': nrm(ks[25], (DEPTH, MIX_DIM, D_MODEL), MIX_DIM ** -0.5),
        'w_router_group': nrm(ks[26], (DEPTH, D_MODEL, N_EXPERT_GROUPS), D_MODEL ** -0.5),
        'b_router_group': nrm(ks[27], (DEPTH, N_EXPERT_GROUPS), 0.01),
        'w_router_expert': nrm(ks[28], (DEPTH, N_EXPERT_GROUPS, D_MODEL, EXPERTS_PER_GROUP), D_MODEL ** -0.5),
        'b_router_expert': nrm(ks[29], (DEPTH, N_EXPERT_GROUPS, EXPERTS_PER_GROUP), 0.01),
        'w_expert_gate': nrm(ks[30], (DEPTH, N_EXPERTS, D_MODEL, D_EXPERT), D_MODEL ** -0.5),
        'w_expert_up': nrm(ks[31], (DEPTH, N_EXPERTS, D_MODEL, D_EXPERT), D_MODEL ** -0.5),
        'w_expert_down': nrm(ks[32], (DEPTH, N_EXPERTS, D_EXPERT, D_MODEL), D_EXPERT ** -0.5),
        'final_norm_g': 1.0 + nrm(ks[33], (D_MODEL,), 0.01),
    }

def reference(x_prompt, x_sample, state_conv, state_ssm_re, state_ssm_im, c_prompt, c_sample,
              w_ada, b_ada, norm1_g, norm2_g, w_in, conv_w, lambda_re, lambda_im, log_dt,
              ssm_b_re, ssm_b_im, ssm_c_re, ssm_c_im, ssm_d, w_glu, b_glu, out_norm_conv_g,
              out_norm_ssm_g, w_out, w_router_group, b_router_group, w_router_expert,
              b_router_expert, w_expert_gate, w_expert_up, w_expert_down, final_norm_g):
    bp = x_prompt.shape[0]
    hp, hs = x_prompt, x_sample
    conv_p, re_p, im_p, conv_s, re_s, im_s = [], [], [], [], [], []
    for l in range(DEPTH):
        lp = (w_ada[l], b_ada[l], norm1_g[l], norm2_g[l], w_in[l], conv_w[l], lambda_re[l],
              lambda_im[l], log_dt[l], ssm_b_re[l], ssm_b_im[l], ssm_c_re[l], ssm_c_im[l], ssm_d[l],
              w_glu[l], b_glu[l], out_norm_conv_g[l], out_norm_ssm_g[l], w_out[l],
              w_router_group[l], b_router_group[l], w_router_expert[l], b_router_expert[l],
              w_expert_gate[l], w_expert_up[l], w_expert_down[l])
        zero_conv = jnp.zeros((bp, CONV_WIDTH - 1, CONV_DIM), x_prompt.dtype)
        zero_ssm = jnp.zeros((bp, SSM_GROUPS, SSM_STATE), x_prompt.dtype)
        hp, cb_p, sr_p, si_p = _layer(hp, c_prompt, zero_conv, zero_ssm, zero_ssm, *lp)
        hs, cb_s, sr_s, si_s = _layer(hs, c_sample, state_conv[l], state_ssm_re[l], state_ssm_im[l], *lp)
        conv_p.append(cb_p); re_p.append(sr_p); im_p.append(si_p)
        conv_s.append(cb_s); re_s.append(sr_s); im_s.append(si_s)
    y_prompt = _rmsnorm(hp, final_norm_g)
    y_sample = _rmsnorm(hs, final_norm_g)
    new_conv_prompt = jnp.stack(conv_p)
    new_ssm_re_prompt = jnp.stack(re_p)
    new_ssm_im_prompt = jnp.stack(im_p)
    new_conv_sample = jnp.stack(conv_s)
    new_ssm_re_sample = jnp.stack(re_s)
    new_ssm_im_sample = jnp.stack(im_s)
    return (y_prompt, y_sample, new_conv_prompt, new_ssm_re_prompt, new_ssm_im_prompt,
            new_conv_sample, new_ssm_re_sample, new_ssm_im_sample)


_drawn_inputs = setup_inputs


def setup_inputs(seed=0):
    import zlib

    import numpy as np

    out = dict(_drawn_inputs(seed))
    spreads = {}
    factors = {'b_ada': 2.679,
     'norm1_g': 4.234,
     'norm2_g': 5.482,
     'lambda_re': 4.019,
     'ssm_c_re': 2.871,
     'b_glu': 8.0,
     'out_norm_conv_g': 8.0,
     'out_norm_ssm_g': 8.0,
     'b_router_group': 6.88,
     'b_router_expert': 8.0,
     'final_norm_g': 5.712}
    for name, (base, spread) in spreads.items():
        noise = np.random.default_rng([zlib.crc32(name.encode()), seed]).standard_normal(out[name].shape)
        drawn = base * np.exp(spread * noise) if base else spread * noise
        out[name] = __import__('jax').numpy.asarray(drawn.astype(out[name].dtype))
    for name, factor in factors.items():
        out[name] = (out[name] * factor).astype(out[name].dtype)
    return out
```

```python
from contextlib import ExitStack
import math

import concourse.bass as bass
from concourse import mybir

F32 = mybir.dt.float32
BF16 = mybir.dt.bfloat16
I32 = mybir.dt.int32
ALU = mybir.AluOpType
ACT = mybir.ActivationFunctionType
AX_X = mybir.AxisListType.X

P = 128
D = 1024
KT = D // P
NP_TOK, NB, NS = 512, 8, 4
NS_TOK = NB * NS
TOK = NP_TOK + NS_TOK
TILES = [(0, 128), (128, 128), (256, 128), (384, 128), (512, 32)]
ROWS = 1 + NB
FT = 4
CH = 8
NC = NP_TOK // CH
YC = NB + NC
UC = YC + NB
GR, GH, ST = 32, 16, 64
NJ = GR // 2
NG, NE_G = 4, 8
NE = NG * NE_G
DE = 256
RANKS = TOK // P + 1
EPS = 1e-6
BIG = 1.0e30
CHUNK = KT * 512
EXPERT = KT * 2 * DE + 2 * D
NBUF = 3
NSLOT = 4
OOB = 4096.0


def KB(k):
    return int(256 * k)


STREAM = ([("ada", c) for c in range(4)] + [("in", c) for c in range(4)]
          + [("ada", c) for c in range(4, 12)] + [("glu", 0), ("out", 0), ("out", 1)])
BLOCK_OF = {name: n for n, name in enumerate(STREAM)}


def bank_jobs():
    jobs = [("ada", c, "v") for c in range(4)] + [("modT", 0, "v")]
    for i in range(4):
        jobs += [("xT", (i, 0), "a"), ("xT", (i, 1), "v")]
    jobs += [("xTs", 0, "v")]
    jobs += [("zu", f, "a") for f in range(FT)] + [("zus", 0, "a")]
    jobs += [("WT", (r, q), "a") for r in range(2) for q in range(4)]
    jobs += [("G", (e, q), "a") for q in range(4) for e in range(2)]
    jobs += [("U1", (f, h), "av"[h]) for f in range(FT) for h in range(2)]
    jobs += [("U2", q, "av"[q % 2]) for q in range(8)]
    jobs += [("S", (r, q), "v") for q in range(4) for r in range(2)]
    jobs += [("zc", f, "a") for f in range(FT)] + [("zcs", 0, "a")]
    jobs += [("zv", f, "v") for f in range(FT)] + [("zvs", 0, "v")]
    jobs += [("zb", f, "v") for f in range(FT)] + [("zbs", 0, "v")]
    jobs += [("ada", c, "v") for c in range(4, 12)]
    jobs += [("Y", (q, e), "a") for q in range(4) for e in range(2)]
    jobs += [("YT", (f, h), "v") for f in range(FT) for h in range(2)]
    jobs += [("gl", m, "a") for m in range(FT)] + [("gls", 0, "a")]
    jobs += [("ss", 0, "v")]
    for i in range(6):
        if i < 5:
            jobs += [(w, (i, n), o) for n in range(2) for w, o in (("mc", "a"), ("ms", "v"))]
        if i > 0:
            jobs += [("hT", (i - 1, 0), "a"), ("hT", (i - 1, 1), "a"), ("rl", i - 1, "v")]
    jobs += [("pos", 0, "v")]
    return jobs


JOBS = bank_jobs()
JOB_OF = {(name, key): n for n, (name, key, _) in enumerate(JOBS)}


def emptied(n):
    owner = JOBS[n][2]
    return owner, sum(o == owner for _, _, o in JOBS[:n + 1])


def build(nc, t):
    ctx = ExitStack()
    with ctx:
        def sem(name):
            return ctx.enter_context(nc.semaphore(name))

        arena = ctx.enter_context(nc.sbuf_tensor("arena", [P, KB(207.5)], F32))
        banks = [ctx.enter_context(nc.psum_tensor(f"bank{b}", [P, 512], F32)) for b in range(8)]

        def at(k, *shape, rows=P, dt=F32):
            n = 1
            for s in shape:
                n *= s
            words = n if dt != BF16 else (n + 1) // 2
            v = arena[0:rows, KB(k):KB(k) + words]
            if dt != F32:
                v = v.bitcast(dt)
            if len(shape) == 1:
                return v
            names = "abcd"[:len(shape)]
            return v.rearrange(f"p ({' '.join(names)}) -> p {' '.join(names)}",
                               **{names[i]: shape[i] for i in range(1, len(shape))})

        block_buf = [at(16 * b, KT, 512) for b in range(NBUF)]
        slot = [at(24 * s, EXPERT) for s in range(NSLOT)]
        slot_in = [s[:, 0:KT * 512].rearrange("p (k n) -> p k n", k=KT) for s in slot]
        slot_down = [s[:, KT * 512:EXPERT].rearrange("p (k n) -> p k n", k=2) for s in slot]
        w_p = [at(48, NJ, CH, GH), at(56, NJ, CH, GH)]
        u_cm = at(48, GR, CH, GH, rows=UC)
        rot_a, rot_b = at(48, NJ, NC), at(52, NJ, NC)
        rot_w = [at(56, NJ, NC), at(60, NJ, NC)]
        g2_row = at(48, D, rows=ROWS)
        mod_out = at(52, 2, 512, rows=ROWS)
        y_cm = at(48, CH, GR, GH, rows=YC)
        g1_row = at(64, D, rows=ROWS)
        X = [at(64, NJ, NB + 1 + NC), at(68.6875, NJ, NB + 1 + NC)]
        mix_t = [at(64, 512), at(66, 512)]
        ada_bias = at(73.5, NBUF, 512, rows=ROWS)
        T = at(80, GR, CH * GH)
        x_tok = at(96, 5, D)
        g_sb = at(96, GR, CH * GH, rows=GH)
        y_conv = at(96, FT, TOK)
        cv_p = at(105, FT, 2 + NP_TOK)
        cv_s = at(113.125, FT, NB, 2 + NS)
        h2T = [at(105, KT, P), at(109, KT, P)]
        hT = at(116, KT, TOK)
        gates = at(116, 4, D)
        WT = [at(133, NJ, P), at(141, NJ, P)]
        gates_s = at(133, 4, D, rows=NS_TOK)
        CA = [at(149, NJ, CH + 1, GH), at(158, NJ, CH + 1, GH)]
        u_ph = at(167, FT, CH, UC)
        x1 = at(149, 5, D)
        fg = at(169, D)
        par = at(177, 2560)
        u_pk = at(177, GR, UC)
        sg = at(177, FT, TOK)
        mod_row = at(187, 2 * D, rows=ROWS)
        E = [at(187, NJ, NC), at(191, NJ, NC)]
        yT = at(187, FT, TOK)
        h2 = [at(187, D), at(191, D)]

        def tmp_at(*shape):
            return at(195, *shape)

        st_s, st_tmp = at(132, 2, NJ, NB), at(114, NJ, NB)
        junk_x, junk_m = at(116, D), at(195.5, D)
        S = [at(195, NJ, UC), at(200, NJ, UC)]
        sq = at(195.5, FT, TOK)
        sqc = at(105, FT, TOK)
        ident = at(205, P)
        small = at(205.5, 512)
        fvec = small[:, 0:FT * 7].rearrange("p (f v) -> p f v", v=7)
        one = small[:, 28:29]
        modT = small[:, 32:32 + 2 * KT * ROWS].rearrange("p (m r) -> p m r", r=ROWS)
        cT = small[:, 176:176 + KT * ROWS].rearrange("p (k r) -> p k r", r=ROWS)
        silT = small[:, 248:248 + KT * ROWS].rearrange("p (k r) -> p k r", r=ROWS)
        a4 = [small[:, 320:336], small[:, 336:352]]
        r8 = small[:, 352:368]
        st_p = small[:, 432:464].rearrange("p (r j) -> p r j", r=2)
        ms = small[:, 384:389]
        rstd = small[:, 389:394]
        ms_m = small[:, 394:404]
        rstd_m = small[:, 404:414]
        half = small[:, 414:424]
        npass = small[:, 424:425].bitcast(I32)
        cnt = small[:, 425:430]
        off = [0]

        def par_at(*shape):
            n = math.prod(shape)
            v = par[:, off[0]:off[0] + n]
            off[0] += n
            if len(shape) > 1:
                ax = "abc"[:len(shape)]
                v = v.rearrange(f"p ({' '.join(ax)}) -> p {' '.join(ax)}",
                                **{ax[i]: shape[i] for i in range(1, len(shape))})
            return v

        lam = par_at(3, NJ)
        lr, li, ldt = lam[:, 0, :], lam[:, 1, :], lam[:, 2, :]
        bc = par_at(4, NJ * GH)
        b_in = [bc[:, r, :].rearrange("p (j h) -> p j h", h=GH) for r in range(2)]
        c_in = [bc[:, 2 + r, :].rearrange("p (j h) -> p j h", h=GH) for r in range(2)]
        bb = [par_at(NJ, GH), par_at(NJ, GH)]
        pw = [par_at(NJ, CH + 1), par_at(NJ, CH + 1)]
        dt_, x_, k_, r_, mag, ang, sin_a, sin_h, cos_a, den, am1, fr, fi = (par_at(NJ) for _ in range(13))
        bits_ = par_at(NJ).bitcast(I32)
        ph = [[par_at(NJ) for i in range(2)] for r in range(2)]
        assert off[0] <= 2560
        wr = at(114.5, KT, NG + NE)
        br = at(115.75, NG + NE)
        logit = at(173, 5, NG + NE)
        ex = at(173.75, 5, NG)
        gm = at(174, 5, 8)
        gone = at(174.25, 5, NG)
        les = at(175.25, 5, NE)
        m1 = at(176, 5, NE)
        m2 = at(96, 5, NE)
        mask = at(96.75, 5, NE)
        mask_b = at(97.5, 5, NE, dt=BF16)
        posm = at(98, 5, NE)
        tri = at(98.75, P, dt=BF16)
        ones_b = at(99, P, dt=BF16)
        iota = at(99.25, P)
        vtok = at(99.75, 5, NE, 2, dt=BF16)
        vt = at(100.5, 5, 4)
        w32 = at(101, NE)
        w4 = at(101.25, NG)
        wk = at(101.5, 5, 2)
        vti = at(101.75, 5, 2, dt=I32)
        tok_id = at(101.875, 5, dt=I32)
        onehot = [at(102, 5, P, dt=BF16), at(103.25, 5, P, dt=BF16)]
        idx = at(104.5, 4, 2, dt=I32)
        idxf = at(104.75, 4)
        xg = [at(105, D), at(109, D)]
        xgT = [at(181, KT, P), at(185, KT, P)]
        yo = [at(189, D), at(193, D)]
        gate_s = [at(197, DE), at(198, DE)]
        he = [at(199, DE), at(200, DE)]
        heT = at(201, 2, P)
        y01 = [at(0, 2, D), at(8, 2, D)]
        acc = [at(16, D), at(20, D)]
        x2 = [at(24, D), at(28, D)]
        junk = at(32, D)

        x_in = [sem(f"x_in{i}") for i in range(5)]
        par_in, conv_in, g2_in, wr_in, x_again = (sem(n) for n in ("par_in", "conv_in", "g2_in", "wr_in", "x_again"))
        block_in = [sem(f"block_in{b}") for b in range(NBUF)]
        bias_in = [sem(f"bias_in{b}") for b in range(NBUF)]
        bank_full = sem("bank_full")
        bank_free = {"a": sem("bank_free_act"), "v": sem("bank_free_dve")}
        dchain, achain, pchain = sem("dve_chain"), sem("act_chain"), sem("pool_chain")
        consts, small_set = sem("consts"), sem("small_set")
        silu_e, sil_ready = sem("silu_exp"), sem("sil_ready")
        ss_x, rstd_ready, xn_ready = sem("ss_x"), sem("rstd_ready"), sem("xn_ready")
        ang_ready, sin_ready = sem("ang_ready"), sem("sin_ready")
        w_ready, ca_ready = sem("w_ready"), sem("ca_ready")
        T_zero, T_built = sem("T_zero"), sem("T_built")
        scan_done, states_ready, state_out = sem("scan_done"), sem("states_ready"), sem("state_out")
        cv_ready, conv_done = sem("cv_ready"), sem("conv_done")
        mod_row_ready = sem("mod_row_ready")
        mod_stored = [sem("mod_stored0"), sem("mod_stored1")]
        gates_in = sem("gates_in")
        yT_ready, gelu_done, ysm_ready = sem("yT_ready"), sem("gelu_done"), sem("ysm_ready")
        sqc_ready, sq_ready, ymix_ready = sem("sqc_ready"), sem("sq_ready"), sem("ymix_ready")
        msm_ready, mrstd_ready = sem("msm_ready"), sem("mrstd_ready")
        mix_a, x1_ready = sem("mix_a"), sem("x1_ready")
        ss_x1, rstd1_ready, h2_ready = sem("ss_x1"), sem("rstd1_ready"), sem("h2_ready")
        h2_stored = [sem("h2_stored0"), sem("h2_stored1")]
        lg_ready, ex_ready, d_ready, dex_ready = sem("lg_ready"), sem("ex_ready"), sem("d_ready"), sem("dex_ready")
        moe_consts, mask_ready, route_ready = sem("moe_consts"), sem("mask_ready"), sem("route_ready")
        slot_full = [sem(f"slot_full{s}") for s in range(NSLOT)]
        oh_ready, idx_done, idx_ready = sem("oh_ready"), sem("idx_done"), sem("idx_ready")
        gathered = [sem("gathered0"), sem("gathered1")]
        scattered = [sem("scattered0"), sem("scattered1")]
        rows_go = sem("rows_go")
        idx_step, h0_in, hs_ready = sem("idx_step"), sem("h0_in"), sem("hs_ready")
        tr_done, xgT_ready = sem("tr_done"), sem("xgT_ready")
        gu_done, gs_ready, he_ready = sem("gu_done"), sem("gs_ready"), sem("he_ready")
        heT_done, heT_ready = sem("heT_done"), sem("heT_ready")
        down_done, yo_ready = sem("down_done"), sem("yo_ready")
        pass_open = sem("pass_open")
        y_in = [sem("y_in0"), sem("y_in1")]
        acc_ready, ss_x2, rstd2_ready = sem("acc_ready"), sem("ss_x2"), sem("rstd2_ready")
        y_ready, y_out = sem("y_ready"), [sem("y_out0"), sem("y_out1")]

        mod_d = nc.dram_tensor("mod_rows", [ROWS, 4, D], F32, kind="Internal").ap()
        h2_d = nc.dram_tensor("h2_rows", [TOK, D], F32, kind="Internal").ap()
        y_d = nc.dram_tensor("expert_rows", [2 * TOK, D], F32, kind="Internal").ap()

        def job(name, key=0):
            return JOB_OF[(name, key)]

        def bank(n):
            return banks[n % 8]

        def wait_full(eng, n):
            eng.wait_ge(bank_full, n + 1)

        def wait_emptied(eng, n):
            owner, count = emptied(n)
            eng.wait_ge(bank_free[owner], count)

        def block_value(n):
            return 16 * (n // NBUF + 1)

        def last_job_of(n):
            kind, c = STREAM[n]
            if kind == "ada":
                return job("ada", c)
            if kind == "in":
                return job(("zus", "zcs", "zvs", "zbs")[c])
            return job("gls") if kind == "glu" else job("ms", (4, c))

        def after(eng, s, p, k):
            if not (isinstance(k, int) and k == 0):
                eng.wait_ge(s, p * NE + k)

        block = ctx.enter_context(nc.Block())

        @block.sync
        def _(sp):
            for i, (t0, n) in enumerate(TILES):
                src = t["x_prompt"][t0:t0 + n, :] if i < 4 else t["x_sample"]
                sp.dma_start(x_tok[0:n, i, :], src).then_inc(x_in[i], 16)
            for n, (kind, c) in enumerate(STREAM):
                b = n % NBUF
                if kind == "ada":
                    if c >= NBUF:
                        wait_emptied(sp, job("ada", c - NBUF))
                    sp.dma_start(ada_bias[:, c % NBUF, :], t["b_ada"][:, 512 * c:512 * c + 512]).then_inc(bias_in[c % NBUF], 16)
                if n >= NBUF:
                    wait_full(sp, last_job_of(n - NBUF))
                kts = FT if kind == "glu" else KT
                src = t["w_glu"] if kind == "glu" else t["w_" + kind][c]
                sp.dma_start(block_buf[b][:, 0:kts, :], src.rearrange("p (k n) -> p k n", k=kts)).then_inc(block_in[b], 16)

            def load_first(sp, mixer_over=None):
                for e in range(NSLOT):
                    s = (e + 3) % NSLOT
                    if e == 1 and mixer_over:
                        mixer_over()
                    sp.dma_start(slot[s], t["w_exp"][e]).then_inc(slot_full[s], 16)

            def load_rest(sp, p):
                with sp.Fori(1, NE // NSLOT) as g:
                    for i in range(NSLOT):
                        s = (i + 3) % NSLOT
                        sp.wait_ge(down_done, p * NE + g * NSLOT + (i - 3))
                        src = t["w_exp"][bass.ds(g * NSLOT + i, 1)].rearrange("e p n -> (e p) n")
                        sp.dma_start(slot[s], src).then_inc(slot_full[s], 16)

            wait_full(sp, job("Y", (3, 1)))
            sp.wait_ge(states_ready, 1)
            load_first(sp, lambda: sp.wait_ge(x1_ready, 10))
            load_rest(sp, 0)
            sp.wait_ge(route_ready, 1)
            passes = sp.value_load(npass[0:1, 0:1], min_val=1, max_val=RANKS)
            with sp.If(passes > 1):
                with sp.Fori(1, passes) as p:
                    sp.wait_ge(pass_open, p + 1)
                    load_first(sp)
                    load_rest(sp, p)

            def store_y(i):
                t0, n = TILES[i]
                sp.wait_ge(y_ready, i + 1)
                dst = t["y_prompt"][t0:t0 + n, :] if i < 4 else t["y_sample"]
                sp.dma_start(dst, x2[i % 2][0:n, :]).then_inc(y_out[i % 2], 16)

            sp.wait_ge(pass_open, passes + 1)
            for i, (t0, n) in enumerate(TILES):
                if i >= 2:
                    sp.wait_ge(acc_ready, i - 1)
                sp.dma_start(y01[i % 2][0:n], y_d[2 * t0:2 * (t0 + n), :].rearrange("(t k) d -> t k d", k=2)).then_inc(y_in[i % 2], 16)
                if i >= 2:
                    store_y(i - 2)
            store_y(3)
            store_y(4)
            sp.wait_ge(y_out[0], 16 * 3)
            sp.wait_ge(y_out[1], 16 * 2)

        @block.gpsimd
        def _(pool):
            def link(ins):
                link.n += 1
                ins.then_inc(pchain, 1)
                pool.wait_ge(pchain, link.n)
            link.n = 0

            def power(out, sums, tmp_, width, done):
                link(pool.tensor_scalar(tmp_, sums, 1.0 / width, EPS, ALU.mult, ALU.add))
                pool.tensor_tensor(out, tmp_, half[0:out.shape[0], 0:out.shape[1]], ALU.pow).then_inc(done, 1)

            link(pool.memset(ident, 0.0))
            pool.affine_select(out=ident, in_=ident, compare_op=ALU.not_equal, fill=1.0, base=0,
                               pattern=[[-1, P]], channel_multiplier=1).then_inc(consts, 1)
            pool.memset(one, 1.0).then_inc(consts, 1)
            pool.memset(small[:, 384:414], 1.0).then_inc(small_set, 1)
            link(pool.memset(half, -0.5))
            pool.memset(u_ph, 0.0).then_inc(consts, 1)
            pool.memset(T, 0.0).then_inc(T_zero, 1)
            pool.wait_ge(ss_x, 5)
            power(rstd, ms, rstd, D, rstd_ready)
            wait_emptied(pool, job("xTs"))
            pool.dma_start(cv_s[:, :, :, 0:2], t["conv_state"]).then_inc(conv_in, 16)
            for r in range(2):
                pool.dma_start(X[r][:, :, 0:NB], t["h0"][r]).then_inc(h0_in, 16)
            pool.wait_ge(T_zero, 1)
            wait_emptied(pool, job("G", (1, 3)))
            for l in range(CH):
                pool.dma_start(T[GH * l:GH * (l + 1), :, GH * l:CH * GH],
                               g_sb[:, :, 0:(CH - l) * GH]).then_inc(T_built, 16)
            pool.wait_ge(scan_done, 1)
            pool.dma_start(g2_row, t["g2"]).then_inc(g2_in, 16)
            pool.dma_start(t["o_ssm_p"], small[:, 432:464]).then_inc(state_out, 16)
            pool.wait_ge(cv_ready, 1)
            pool.dma_start(t["o_conv_p"], cv_p[:, :, NP_TOK:NP_TOK + 2]).then_inc(state_out, 16)
            pool.dma_start(t["o_conv_s"], cv_s[:, :, :, NS:NS + 2]).then_inc(state_out, 16)
            for c in range(4, 12):
                v, h = (c - 4) // 2, c % 2
                pool.wait_ge(mod_row_ready, c + 1)
                pool.dma_start(mod_d[:, v, 512 * h:512 * h + 512], mod_out[:, h, :]).then_inc(mod_stored[h], 16)
            for h in range(2):
                pool.wait_ge(mod_stored[h], 64)
            rows = mod_d.rearrange("r v n -> r (v n)")
            flat = gates.rearrange("p v n -> p (v n)")
            flat_s = gates_s.rearrange("p v n -> p (v n)")
            pool.dma_start(flat, rows[0:1, :].partition_broadcast(P)).then_inc(gates_in, 16)
            for b in range(NB):
                pool.dma_start(flat_s[NS * b:NS * (b + 1), :],
                               rows[1 + b:2 + b, :].partition_broadcast(NS)).then_inc(gates_in, 16)
            pool.wait_ge(states_ready, 1)
            pool.dma_start(t["o_ssm_s"], st_s.rearrange("p r j b -> p (r j b)")).then_inc(state_out, 16)
            pool.wait_ge(yT_ready, FT)
            for i, (t0, n) in enumerate(TILES):
                src = t["x_prompt"][t0:t0 + n, :] if i < 4 else t["x_sample"]
                pool.dma_start(x1[0:n, i, :], src).then_inc(x_again, 16)
            pool.dma_start(fg, t["final_g"]).then_inc(x_again, 16)
            pool.dma_start(wr, t["w_router"]).then_inc(wr_in, 16)
            pool.dma_start(br, t["b_router"]).then_inc(wr_in, 16)
            pool.wait_ge(msm_ready, 1)
            pool.tensor_tensor(rstd_m, ms_m, half, ALU.pow).then_inc(mrstd_ready, 1)
            for i, (t0, n) in enumerate(TILES):
                pool.wait_ge(ss_x1, i + 1)
                power(rstd[0:n, i:i + 1], ms[0:n, i:i + 1], ms[0:n, i:i + 1], D, rstd1_ready)
                pool.wait_ge(h2_ready, i + 1)
                pool.dma_start(h2_d[t0:t0 + n, :], h2[i % 2][0:n, :]).then_inc(h2_stored[i % 2], 16)
            pool.wait_ge(x1_ready, 10)
            link(pool.memset(tri, 1.0))
            link(pool.affine_select(out=tri, in_=tri, compare_op=ALU.is_gt, fill=0.0, base=0,
                                    pattern=[[1, P]], channel_multiplier=-1))
            link(pool.memset(ones_b, 1.0))
            for out, pattern, base, mult in ((iota, [[1, P]], 0, 0), (w32, [[-1, NE]], NE, 0),
                                             (w4, [[-1, NG]], NG, 0), (tok_id, [[P, 5]], 0, 1)):
                link(pool.iota(out, pattern=pattern, base=base, channel_multiplier=mult,
                               allow_small_or_imprecise_dtypes=True))
            pool.sem_inc(moe_consts, 1)
            wait_full(pool, job("rl", 4))
            for b in range(2):
                link(pool.memset(xg[b], 0.0))
            pool.wait_ge(h2_stored[0], 16 * 3)
            pool.wait_ge(h2_stored[1], 16 * 2)
            pool.wait_ge(route_ready, 1)
            passes = pool.value_load(npass[0:1, 0:1], min_val=1, max_val=RANKS)

            def gather(p, k, n):
                pool.wait_ge(idx_ready, p * NE + k + 1)
                if not (isinstance(k, int) and k < 2):
                    pool.wait_ge(tr_done, p * NE + k - 1)
                pool.sem_inc(rows_go, 1)
                pool.indirect_dma_start(
                    out=xg[n % 2], out_offset=None, in_=h2_d[:, :],
                    in_offset=bass.IndirectOffsetOnAxis(ap=idx[:, n % 4, 1:2], axis=0),
                    bounds_check=TOK - 1, oob_is_err=False).then_inc(gathered[n % 2], 16)

            def scatter(p, k, n):
                pool.wait_ge(yo_ready, p * NE + k + 1)
                pool.sem_inc(rows_go, 1)
                pool.indirect_dma_start(
                    out=y_d[:, :], in_=yo[n % 2], in_offset=None,
                    out_offset=bass.IndirectOffsetOnAxis(ap=idx[:, n % 4, 0:1], axis=0),
                    bounds_check=2 * TOK - 1, oob_is_err=False).then_inc(scattered[n % 2], 16)

            with pool.Fori(0, passes) as p:
                for n in range(4):
                    gather(p, n, n)
                    if n >= 2:
                        scatter(p, n - 2, n - 2)
                with pool.Fori(1, NE // 4) as g:
                    for n in range(4):
                        gather(p, g * 4 + n, n)
                        scatter(p, g * 4 + (n - 2), n + 2)
                for n in (NE - 2, NE - 1):
                    scatter(p, n, n)
            for i, (t0, n) in enumerate(TILES):
                pool.wait_ge(ss_x2, i + 1)
                power(rstd[0:n, i:i + 1], ms[0:n, i:i + 1], ms[0:n, i:i + 1], D, rstd2_ready)
            pool.wait_ge(state_out, 16 * 4)

        @block.scalar
        def _(act):
            def link(ins):
                link.n += 1
                ins.then_inc(achain, 1)
                act.wait_ge(achain, link.n)
            link.n = 0

            def done(ins):
                ins.then_inc(bank_free["a"], 1)

            loads = [(cT, "cT"), (lam, "lam"), (bc, "bc"), (fvec, "fvec"), (g1_row, "g1")]
            for dst, src in loads:
                act.dma_start(dst, t[src]).then_inc(par_in, 16)
            act.wait_ge(par_in, 16 * len(loads))
            nc.scalar.activation(silT, cT, ACT.Exp, scale=-1.0).then_inc(silu_e, 1)
            act.wait_ge(small_set, 1)
            for i, (t0, n) in enumerate(TILES):
                act.wait_ge(x_in[i], 16)
                if i > 0:
                    act.wait_ge(ss_x, i)
                nc.scalar.activation(junk_x[0:n, :], x_tok[0:n, i, :], ACT.Square,
                                     accum_out=ms[0:n, i:i + 1]).then_inc(ss_x, 1)
            act.wait_ge(ang_ready, 1)
            nc.scalar.activation(sin_a, ang, ACT.Sin).then_inc(sin_ready, 1)
            nc.scalar.activation(sin_h, ang, ACT.Sin, scale=0.5).then_inc(sin_ready, 1)
            wait_emptied(act, job("modT"))
            act.wait_ge(ss_x, 5)
            for i in range(4):
                n = job("xT", (i, 0))
                wait_full(act, n)
                for k in range(4):
                    ins = nc.scalar.activation(hT[:, k, P * i:P * (i + 1)], bank(n)[:, P * k:P * (k + 1)],
                                               ACT.Identity, bias=modT[:, k, 0:1], scale=modT[:, KT + k, 0:1])
                done(ins)
            act.wait_ge(consts, 3)
            for f in range(FT):
                n = job("zu", f)
                wait_full(act, n)
                done(nc.scalar.activation(u_ph[:, f, :, NB:YC],
                                          bank(n)[:, :].rearrange("p (c l) -> p l c", l=CH), ACT.Copy))
            n = job("zus")
            wait_full(act, n)
            src = bank(n)[:, 0:FT * NS_TOK].rearrange("p (f b s) -> p f s b", f=FT, b=NB)
            for f in range(FT):
                nc.scalar.activation(u_ph[:, f, 0:NS, 0:NB], src[:, f], ACT.Copy)
                ins = nc.scalar.activation(u_ph[:, f, CH - NS:CH, YC:UC], src[:, f], ACT.Copy)
            done(ins)
            for r in range(2):
                for q in range(4):
                    n = job("WT", (r, q))
                    wait_full(act, n)
                    done(nc.scalar.activation(WT[r][:, 4 * q:4 * q + 4, :].rearrange("p j n -> p (j n)"),
                                              bank(n)[:, :], ACT.Copy))
            wait_emptied(act, job("xTs"))
            for q in range(4):
                for e in range(2):
                    n = job("G", (e, q))
                    wait_full(act, n)
                    done(nc.scalar.activation(g_sb[:, 8 * q + e:8 * q + 8:2, :],
                                              bank(n)[0:GH, :].rearrange("p (j n) -> p j n", j=4), ACT.Copy))
            for f in range(FT):
                n = job("U1", (f, 0))
                wait_full(act, n)
                done(nc.scalar.activation(u_cm[:, 8 * f:8 * f + 8, 0:4, :],
                                          bank(n)[0:UC, :].rearrange("p (l g h) -> p g l h", l=4, g=8), ACT.Copy))
            for q in range(0, 8, 2):
                n = job("U2", q)
                wait_full(act, n)
                done(nc.scalar.activation(u_pk[:, 4 * q:4 * q + 4, :],
                                          bank(n)[:, 0:4 * UC].rearrange("p (g c) -> p g c", g=4), ACT.Copy))
            act.wait_ge(T_built, 16 * CH)
            for f in range(FT):
                n = job("zc", f)
                wait_full(act, n)
                done(nc.scalar.activation(y_conv[:, f, 0:NP_TOK], bank(n)[:, :], ACT.Copy))
            n = job("zcs")
            wait_full(act, n)
            done(nc.scalar.activation(y_conv[:, :, NP_TOK:TOK],
                                      bank(n)[:, 0:FT * NS_TOK].rearrange("p (f n) -> p f n", f=FT), ACT.Copy))
            act.wait_ge(conv_done, 1)
            act.wait_ge(state_out, 16 * 3)
            nc.scalar.activation(sqc, y_conv, ACT.Square).then_inc(sqc_ready, 1)
            for h in range(2):
                act.wait_ge(mod_stored[h], 64)
            for q in range(4):
                for e in range(2):
                    n = job("Y", (q, e))
                    wait_full(act, n)
                    done(nc.scalar.activation(y_cm[:, :, 8 * q + e:8 * q + 8:2, :].rearrange("p l g h -> p g l h"),
                                              bank(n)[0:YC, :].rearrange("p (g l h) -> p g l h", g=4, l=CH), ACT.Copy))
            for f in range(FT):
                act.wait_ge(yT_ready, f + 1)
                nc.scalar.activation(yT[:, f, :], yT[:, f, :], ACT.Gelu_apprx_tanh).then_inc(gelu_done, 1)
            for m in range(FT):
                n = job("gl", m)
                wait_full(act, n)
                done(nc.scalar.activation(sg[:, m, 0:NP_TOK], bank(n)[:, :], ACT.Sigmoid, bias=fvec[:, m, 1:2]))
            n = job("gls")
            wait_full(act, n)
            for m in range(FT):
                ins = nc.scalar.activation(sg[:, m, NP_TOK:TOK], bank(n)[:, NS_TOK * m:NS_TOK * (m + 1)],
                                           ACT.Sigmoid, bias=fvec[:, m, 1:2])
            done(ins)
            act.wait_ge(ysm_ready, 1)
            nc.scalar.activation(sq, sg, ACT.Square).then_inc(sq_ready, 1)

            act.wait_ge(mrstd_ready, 1)
            for i in range(6):
                if i < 5:
                    rows = TILES[i][1]
                    for h in range(2):
                        n = job("mc", (i, h))
                        wait_full(act, n)
                        if i > 0:
                            act.wait_ge(x1_ready, 2 * i - 1 + h)
                        ins = nc.scalar.activation(mix_t[h][0:rows, :], bank(n)[0:rows, :], ACT.Copy,
                                                   scale=rstd_m[0:rows, i:i + 1])
                        done(ins)
                    act.wait_ge(x1_ready, 2 * i + 2)
                    if i > 0:
                        act.wait_ge(rstd1_ready, i)
                    nc.scalar.activation(junk_m[0:rows, :], x1[0:rows, i, :], ACT.Square,
                                         accum_out=ms[0:rows, i:i + 1]).then_inc(ss_x1, 1)
                if i > 0:
                    rows = TILES[i - 1][1]
                    if i > 2:
                        wait_full(act, job("rl", i - 3))
                    for h in range(2):
                        n = job("hT", (i - 1, h))
                        wait_full(act, n)
                        done(nc.scalar.activation(h2T[(i - 1) % 2][:, 4 * h:4 * h + 4, 0:rows],
                                                  bank(n)[:, :].rearrange("p (k n) -> p k n", k=4)[:, :, 0:rows], ACT.Copy))
            act.wait_ge(lg_ready, 1)
            nc.scalar.activation(ex, ex, ACT.Exp).then_inc(ex_ready, 1)
            act.wait_ge(d_ready, 1)
            nc.scalar.activation(wk[:, :, 0:1], wk[:, :, 0:1], ACT.Exp).then_inc(dex_ready, 1)

            act.wait_ge(route_ready, 1)
            passes = act.value_load(npass[0:1, 0:1], min_val=1, max_val=RANKS)

            def x_out(p, k, n):
                act.wait_ge(tr_done, p * NE + k + 1)
                if not (isinstance(k, int) and k < 2):
                    act.wait_ge(gu_done, p * NE + k - 1)
                nc.scalar.activation(xgT[n % 2][:, 0:4, :].rearrange("p k n -> p (k n)"), banks[0][:, :], ACT.Copy)
                nc.scalar.activation(xgT[n % 2][:, 4:8, :].rearrange("p k n -> p (k n)"), banks[1][:, :], ACT.Copy).then_inc(xgT_ready, 1)

            def silu(p, k, n):
                act.wait_ge(gu_done, p * NE + k + 1)
                if not (isinstance(k, int) and k < 2):
                    act.wait_ge(he_ready, p * NE + k - 1)
                nc.scalar.activation(gate_s[n % 2], banks[2 + n % 2][:, 0:DE], ACT.Silu).then_inc(gs_ready, 1)

            def heT_out(p, k):
                act.wait_ge(heT_done, p * NE + k + 1)
                nc.scalar.activation(heT.rearrange("p k n -> p (k n)"), banks[4][:, 0:2 * P], ACT.Copy).then_inc(heT_ready, 1)

            def step(p, k, n, first=False, last=False):
                if not first:
                    heT_out(p, k - 1)
                silu(p, k, n)
                if not last:
                    x_out(p, k + 1, n + 1)

            with act.Fori(0, passes) as p:
                act.wait_ge(pass_open, p + 1)
                x_out(p, 0, 0)
                for n in range(4):
                    step(p, n, n, first=(n == 0))
                with act.Fori(1, NE // 4 - 1) as g:
                    for n in range(4):
                        step(p, g * 4 + n, n)
                for n in range(NE - 4, NE):
                    step(p, n, n, last=(n == NE - 1))
                heT_out(p, NE - 1)
            for i, (t0, n) in enumerate(TILES):
                act.wait_ge(acc_ready, i + 1)
                if i > 0:
                    act.wait_ge(ss_x2, i)
                nc.scalar.activation(junk[0:n, :], x1[0:n, i, :], ACT.Square, accum_out=ms[0:n, i:i + 1]).then_inc(ss_x2, 1)

        @block.vector
        def _(dve):
            V = nc.vector

            def link(ins):
                link.n += 1
                ins.then_inc(dchain, 1)
                dve.wait_ge(dchain, link.n)
            link.n = 0

            def done(ins):
                done.n += 1
                ins.then_inc(bank_free["v"], 1)
                dve.wait_ge(bank_free["v"], done.n)
            done.n = 0

            def tt(out, a, b, op):
                link(V.tensor_tensor(out, a, b, op))

            def ts(out, a, s1, op0, s2=None, op1=None):
                if op1 is None:
                    link(V.tensor_scalar(out, a, s1, None, op0))
                else:
                    link(V.tensor_scalar(out, a, s1, s2, op0, op1))

            def stt(out, a, s, b, op0, op1):
                link(V.scalar_tensor_tensor(out=out, in0=a, scalar=s, in1=b, op0=op0, op1=op1))

            def cmul(o, a, b, tmp_, conj=False, neg_im=False):
                tt(o[0], a[0], b[0], ALU.mult)
                tt(tmp_, a[1], b[1], ALU.mult)
                tt(o[0], o[0], tmp_, ALU.add if conj else ALU.subtract)
                tt(o[1], a[0], b[1], ALU.mult)
                tt(tmp_, a[1], b[0], ALU.mult)
                if neg_im:
                    stt(o[1], o[1], -1.0, tmp_, ALU.mult, ALU.subtract)
                else:
                    tt(o[1], o[1], tmp_, ALU.subtract if conj else ALU.add)

            MAGIC = 1.5 * 2.0 ** 23

            def exp_exact(out, x, k, r, bits):
                ts(k, x, 1.0 / math.log(2.0), ALU.mult, MAGIC, ALU.add)
                ts(k, k, -MAGIC, ALU.add, -126.0, ALU.max)
                ts(k, k, 127.0, ALU.min)
                stt(r, k, -0.693359375, x, ALU.mult, ALU.add)
                stt(r, k, 2.12194440e-4, r, ALU.mult, ALU.add)
                ts(out, r, 1.0 / 5040.0, ALU.mult)
                for c in (720.0, 120.0, 24.0, 6.0, 2.0, 1.0):
                    stt(out, out, 1.0 / c, r, ALU.add, ALU.mult)
                ts(bits, k, 127.0, ALU.add, 2.0 ** 23, ALU.mult)
                stt(out, out, 1.0, bits.bitcast(F32), ALU.add, ALU.mult)

            def bc3(v, shape):
                for _ in range(len(shape) - v.ndim):
                    v = v.unsqueeze(v.ndim)
                return v.to_broadcast(shape)

            dve.wait_ge(silu_e, 1)
            ts(silT, silT, 1.0, ALU.add)
            link(V.reciprocal(silT, silT))
            V.tensor_tensor(silT, silT, cT, ALU.mult).then_inc(sil_ready, 1)
            exp_exact(dt_, ldt, k_, r_, bits_)
            tt(x_, lr, dt_, ALU.mult)
            exp_exact(mag, x_, k_, r_, bits_)
            tt(x_, li, dt_, ALU.mult)
            ts(k_, x_, 1.0 / (2.0 * math.pi), ALU.mult, MAGIC, ALU.add)
            ts(k_, k_, -MAGIC, ALU.add)
            stt(ang, k_, -6.28125, x_, ALU.mult, ALU.add)
            stt(ang, k_, -0.0019353071795864769, ang, ALU.mult, ALU.add)
            V.tensor_scalar(ang, ang, 3.1415925, -3.1415925, ALU.min, ALU.max).then_inc(ang_ready, 1)
            dve.wait_ge(rstd_ready, 1)
            for i, (t0, n) in enumerate(TILES):
                V.tensor_scalar(x_tok[0:n, i, :], x_tok[0:n, i, :], rstd[0:n, i:i + 1], None, ALU.mult).then_inc(xn_ready, 1)
            dve.wait_ge(sin_ready, 2)
            tt(cos_a, sin_h, sin_h, ALU.mult)
            ts(cos_a, cos_a, -2.0, ALU.mult, 1.0, ALU.add)
            a = [pw[0][:, :, 1], pw[1][:, :, 1]]
            tt(a[0], mag, cos_a, ALU.mult)
            tt(a[1], mag, sin_a, ALU.mult)
            link(V.memset(pw[0][:, :, 0:1], 1.0))
            link(V.memset(pw[1][:, :, 0:1], 0.0))
            for have in (1, 2, 4):
                top = [bc3(pw[r][:, :, have], [P, NJ, have]) for r in range(2)]
                cmul([pw[r][:, :, have + 1:2 * have + 1] for r in range(2)], top,
                     [pw[r][:, :, 1:have + 1] for r in range(2)], tmp_at(NJ, have))
            for r in range(2):
                link(V.tensor_copy(a4[r], pw[r][:, :, 4]))
            tt(den, lr, lr, ALU.mult)
            tt(x_, li, li, ALU.mult)
            tt(den, den, x_, ALU.add)
            link(V.reciprocal(den, den))
            ts(am1, a[0], -1.0, ALU.add)
            cmul([fr, fi], [lr, li], [am1, a[1]], x_, conj=True)
            tt(fr, fr, den, ALU.mult)
            tt(fi, fi, den, ALU.mult)
            cmul(bb, [bc3(fr, [P, NJ, GH]), bc3(fi, [P, NJ, GH])], b_in, tmp_at(NJ, GH))
            for l in range(CH):
                cmul([w_p[r][:, :, l, :] for r in range(2)],
                     [bc3(pw[r][:, :, CH - 1 - l], [P, NJ, GH]) for r in range(2)], bb, tmp_at(NJ, GH))
            dve.sem_inc(w_ready, 1)

            def ada_rows(c):
                n = job("ada", c)
                wait_full(dve, n)
                dve.wait_ge(bias_in[c % NBUF], 16 * (c // NBUF + 1))
                h = c % 2
                if c < 4:
                    out = mod_row[:, 512 * c:512 * c + 512]
                else:
                    out = mod_out[:, h, :]
                    if c >= 6:
                        dve.wait_ge(mod_stored[h], 16 * ((c - 4) // 2))
                done(V.tensor_tensor(out, bank(n)[0:ROWS, :], ada_bias[:, c % NBUF, :], ALU.add))
                if c in (2, 3):
                    stt(out, out, 1.0, g1_row[:, 512 * h:512 * h + 512], ALU.add, ALU.mult)
                if c in (8, 9):
                    dve.wait_ge(g2_in, 16)
                    stt(out, out, 1.0, g2_row[:, 512 * h:512 * h + 512], ALU.add, ALU.mult)
                dve.sem_inc(mod_row_ready, 1)

            dve.wait_ge(par_in, 16 * 5)
            for c in range(4):
                ada_rows(c)
            n = job("modT")
            wait_full(dve, n)
            done(V.tensor_copy(modT, bank(n)[:, 0:2 * KT * ROWS].rearrange("p (m r) -> p m r", r=ROWS)))
            for i in range(4):
                n = job("xT", (i, 1))
                wait_full(dve, n)
                for k in range(4, KT):
                    ins = V.tensor_scalar(hT[:, k, P * i:P * (i + 1)], bank(n)[:, P * (k - 4):P * (k - 3)],
                                          modT[:, KT + k, 0:1], modT[:, k, 0:1], ALU.mult, ALU.add)
                    if k < KT - 1:
                        link(ins)
                done(ins)
            n = job("xTs")
            wait_full(dve, n)
            hs = hT[:, :, NP_TOK:TOK].rearrange("p k (b s) -> p k b s", s=NS)
            ps = bank(n)[:, 0:KT * NS_TOK].rearrange("p (k b s) -> p k b s", k=KT, b=NB)
            for k in range(KT):
                sc_ = modT[:, KT + k, 1:ROWS].unsqueeze(2).to_broadcast([P, NB, NS])
                ins = V.tensor_tensor(hs[:, k], ps[:, k], sc_, ALU.mult)
                if k < KT - 1:
                    link(ins)
            done(ins)
            for k in range(KT):
                sh_ = modT[:, k, 1:ROWS].unsqueeze(2).to_broadcast([P, NB, NS])
                tt(hs[:, k], hs[:, k], sh_, ALU.add)
            dve.sem_inc(hs_ready, 1)

            for d in range(CH + 1):
                cmul([CA[r][:, :, d, :] for r in range(2)],
                     [bc3(pw[r][:, :, d], [P, NJ, GH]) for r in range(2)], c_in, tmp_at(NJ, GH), neg_im=True)
            dve.sem_inc(ca_ready, 1)
            cur = [cos_a, sin_a]
            for o in (ph[0], ph[1], ph[0]):
                cmul(o, cur, cur, x_)
                cur = o
            link(V.memset(E[0][:, :, 0:1], 1.0))
            link(V.memset(E[1][:, :, 0:1], 0.0))
            have = 1
            while have < NC:
                cmul([E[r][:, :, have:2 * have] for r in range(2)],
                     [bc3(cur[r], [P, NJ, have]) for r in range(2)],
                     [E[r][:, :, 0:have] for r in range(2)], tmp_at(NJ, have))
                nxt = ph[1] if cur is ph[0] else ph[0]
                cmul(nxt, cur, cur, x_)
                cur = nxt
                have *= 2
            tt(r8, mag, mag, ALU.mult)
            tt(r8, r8, r8, ALU.mult)
            tt(r8, r8, r8, ALU.mult)

            for f in range(FT):
                n = job("U1", (f, 1))
                wait_full(dve, n)
                wait_emptied(dve, job("WT", (1, 3)))
                done(V.tensor_copy(u_cm[:, 8 * f:8 * f + 8, 4:8, :],
                                   bank(n)[0:UC, :].rearrange("p (l g h) -> p g l h", l=4, g=8)))
            for q in range(1, 8, 2):
                n = job("U2", q)
                wait_full(dve, n)
                done(V.tensor_copy(u_pk[:, 4 * q:4 * q + 4, :], bank(n)[:, 0:4 * UC].rearrange("p (g c) -> p g c", g=4)))
            for q in range(4):
                for r in range(2):
                    n = job("S", (r, q))
                    wait_full(dve, n)
                    done(V.tensor_copy(S[r][:, 4 * q:4 * q + 4, :], bank(n)[:, 0:4 * UC].rearrange("p (j c) -> p j c", j=4)))
            Sp = [S[r][:, :, NB:YC] for r in range(2)]
            cmul(rot_w, E, Sp, rot_a, conj=True)
            link(V.tensor_copy(rot_a, bc3(r8, [P, NJ, NC])))
            link(V.memset(rot_a[:, :, 0:1], 0.0))
            for r in range(2):
                flat = rot_w[r].rearrange("p j c -> p (j c)")
                link(V.tensor_tensor_scan(flat, rot_a.rearrange("p j c -> p (j c)"), flat, 0.0, ALU.mult, ALU.add))
            dve.wait_ge(h0_in, 32)
            cmul([X[r][:, :, NB + 1:] for r in range(2)], E, rot_w, rot_b)
            for r in range(2):
                link(V.memset(X[r][:, :, NB:NB + 1], 0.0))
            for r in range(2):
                link(V.tensor_copy(st_p[:, r], X[r][:, :, NB + NC]))
            dve.sem_inc(scan_done, 1)

            dve.wait_ge(T_built, 16 * CH)
            link(V.memset(cv_p[:, :, 0:2], 0.0))
            wait_emptied(dve, job("zcs"))
            for f in range(FT):
                n = job("zv", f)
                wait_full(dve, n)
                done(V.tensor_tensor(cv_p[:, f, 2:], bank(n)[:, :], y_conv[:, f, 0:NP_TOK], ALU.mult))
            n = job("zvs")
            wait_full(dve, n)
            samples = y_conv[:, :, NP_TOK:TOK].rearrange("p f (b s) -> p f b s", s=NS)
            for f in range(FT):
                ins = V.tensor_tensor(cv_s[:, f, :, 2:], bank(n)[:, NS_TOK * f:NS_TOK * (f + 1)].rearrange("p (b s) -> p b s", s=NS),
                                      samples[:, f], ALU.mult)
                if f < FT - 1:
                    link(ins)
            done(ins)
            dve.wait_ge(conv_in, 16)
            dve.sem_inc(cv_ready, 1)
            for f in range(FT):
                for out, src in ((y_conv[:, f, 0:NP_TOK], lambda k: cv_p[:, f, k:k + NP_TOK]),
                                 (samples[:, f], lambda k: cv_s[:, f, :, k:k + NS])):
                    ts(out, src(0), fvec[:, f, 4:5], ALU.mult)
                    for k in (1, 2):
                        stt(out, src(k), fvec[:, f, 4 + k:5 + k], out, ALU.mult, ALU.add)
            for f in range(FT):
                n = job("zb", f)
                wait_full(dve, n)
                done(V.tensor_tensor(y_conv[:, f, 0:NP_TOK], bank(n)[:, :], y_conv[:, f, 0:NP_TOK], ALU.mult))
            n = job("zbs")
            wait_full(dve, n)
            done(V.tensor_tensor(y_conv[:, :, NP_TOK:TOK], bank(n)[:, 0:FT * NS_TOK].rearrange("p (f n) -> p f n", f=FT),
                                 y_conv[:, :, NP_TOK:TOK], ALU.mult))
            dve.sem_inc(conv_done, 1)
            for c in range(4, 12):
                ada_rows(c)
            a4b = [bc3(a4[r], [P, NJ, NB]) for r in range(2)]
            cmul([st_s[:, r] for r in range(2)], a4b, [X[r][:, :, 0:NB] for r in range(2)], st_tmp)
            for r in range(2):
                tt(st_s[:, r], st_s[:, r], S[r][:, :, YC:UC], ALU.add)
            dve.sem_inc(states_ready, 1)

            for f in range(FT):
                for h in range(2):
                    n = job("YT", (f, h))
                    wait_full(dve, n)
                    pv = bank(n)[:, 0:4 * YC].rearrange("p (l c) -> p l c", l=4)
                    ls = slice(4 * h, 4 * h + 4)
                    if h == 0:
                        link(V.scalar_tensor_tensor(
                            out=yT[:, f, NP_TOK:TOK].rearrange("p (b s) -> p s b", s=NS), in0=u_ph[:, f, 0:NS, 0:NB],
                            scalar=fvec[:, f, 0:1], in1=pv[:, :, 0:NB], op0=ALU.mult, op1=ALU.add))
                    done(V.scalar_tensor_tensor(
                        out=yT[:, f, 0:NP_TOK].rearrange("p (c l) -> p l c", l=CH)[:, ls], in0=u_ph[:, f, ls, NB:YC],
                        scalar=fvec[:, f, 0:1], in1=pv[:, :, NB:YC], op0=ALU.mult, op1=ALU.add))
                dve.sem_inc(yT_ready, 1)
            dve.wait_ge(sqc_ready, 1)
            for f in range(FT):
                ts(y_conv[:, f, :], y_conv[:, f, :], fvec[:, f, 2:3], ALU.mult)
            wait_emptied(dve, job("gls"))
            tt(sg, sg, yT, ALU.mult)
            dve.sem_inc(ysm_ready, 1)
            dve.wait_ge(sq_ready, 1)
            for f in range(FT):
                ts(sg[:, f, :], sg[:, f, :], fvec[:, f, 3:4], ALU.mult)
            dve.sem_inc(ymix_ready, 1)
            n = job("ss")
            wait_full(dve, n)
            pv = bank(n)[:, 0:10].rearrange("p (w i) -> p w i", w=2)
            mv = ms_m.rearrange("p (w i) -> p w i", w=2)
            ts(mv[:, :, 0:4], pv[:, :, 0:4], 1.0 / (FT * P), ALU.mult, EPS, ALU.add)
            done(V.tensor_scalar(mv[0:NS_TOK, :, 4:5], pv[0:NS_TOK, :, 4:5], 1.0 / (FT * P), EPS, ALU.mult, ALU.add))
            dve.sem_inc(msm_ready, 1)

            dve.wait_ge(mrstd_ready, 1)
            dve.wait_ge(gates_in, 16 * (1 + NB))
            dve.wait_ge(x_again, 16 * 6)
            link(V.memset(logit, 0.0))
            dve.wait_ge(wr_in, 32)
            for i in range(6):
                if i < 5:
                    rows = TILES[i][1]
                    gt = gates if i < 4 else gates_s
                    for h in range(2):
                        n = job("ms", (i, h))
                        wait_full(dve, n)
                        wait_emptied(dve, job("mc", (i, h)))
                        cols = slice(512 * h, 512 * h + 512)
                        m = mix_t[h][0:rows, :]
                        done(V.scalar_tensor_tensor(out=m, in0=bank(n)[0:rows, :], scalar=rstd_m[0:rows, 5 + i:6 + i],
                                                    in1=m, op0=ALU.mult, op1=ALU.add))
                        tt(m, m, gt[0:rows, 0, cols], ALU.mult)
                        V.tensor_tensor(x1[0:rows, i, cols], x1[0:rows, i, cols], m, ALU.add).then_inc(x1_ready, 1)
                    if i >= 2:
                        dve.wait_ge(h2_stored[i % 2], 16 * (i // 2))
                        wait_full(dve, job("hT", (i - 2, 1)))
                    else:
                        wait_full(dve, job("ss"))
                    dve.wait_ge(rstd1_ready, i + 1)
                    hv = h2[i % 2][0:rows, :]
                    stt(hv, x1[0:rows, i, :], rstd[0:rows, i:i + 1], gt[0:rows, 2, :], ALU.mult, ALU.mult)
                    V.tensor_tensor(hv, hv, gt[0:rows, 1, :], ALU.add).then_inc(h2_ready, 1)
                if i > 0:
                    n = job("rl", i - 1)
                    rows = TILES[i - 1][1]
                    wait_full(dve, n)
                    done(V.tensor_tensor(logit[0:rows, i - 1, :], bank(n)[0:rows, 0:NG + NE], br[0:rows, :], ALU.add))

            dve.wait_ge(moe_consts, 1)
            col = lambda c: gm[:, :, c:c + 1]
            wide = lambda c, w: col(c).to_broadcast([P, 5, w])
            lg, le = logit[:, :, 0:NG], logit[:, :, NG:NG + NE]
            link(V.tensor_reduce(col(0), lg, AX_X, ALU.max))
            V.tensor_tensor(ex, lg, wide(0, NG), ALU.subtract).then_inc(lg_ready, 1)

            def first_of(out, vals, top, weights, tie, w):
                tt(out, vals, wide(top, w), ALU.is_equal)
                tt(out, out, weights.unsqueeze(1).to_broadcast([P, 5, w]), ALU.mult)
                link(V.tensor_reduce(col(tie), out, AX_X, ALU.max))
                tt(out, out, wide(tie, w), ALU.is_equal)

            first_of(gone, lg, 0, w4, 1, NG)
            ts(gone, gone, BIG, ALU.mult, -BIG, ALU.add)
            tt(les.rearrange("p i (g e) -> p i g e", g=NG), le.rearrange("p i (g e) -> p i g e", g=NG),
               gone.unsqueeze(3).to_broadcast([P, 5, NG, NE_G]), ALU.add)
            link(V.tensor_reduce(col(2), les, AX_X, ALU.max))
            first_of(m1, les, 2, w32, 3, NE)
            stt(les, m1, -BIG, les, ALU.mult, ALU.add)
            link(V.tensor_reduce(col(4), les, AX_X, ALU.max))
            first_of(m2, les, 4, w32, 5, NE)
            V.tensor_tensor(wk[:, :, 0:1], col(4), col(2), ALU.subtract).then_inc(d_ready, 1)
            tt(mask, m1, m2, ALU.add)
            link(V.memset(mask[32:64, 4, :], 0.0))
            link(V.memset(mask[64:128, 4, :], 0.0))
            V.tensor_copy(mask_b, mask).then_inc(mask_ready, 1)
            dve.wait_ge(ex_ready, 1)
            link(V.tensor_reduce(col(6), ex, AX_X, ALU.add))
            dve.wait_ge(dex_ready, 1)
            ts(col(7), wk[:, :, 0:1], 1.0, ALU.add)
            tt(col(6), col(6), col(7), ALU.mult)
            link(V.reciprocal(col(6), col(6)))
            tt(wk[:, :, 1:2], wk[:, :, 0:1], col(6), ALU.mult)
            link(V.tensor_copy(wk[:, :, 0:1], col(6)))
            link(V.tensor_scalar(vti[:, :, 0], tok_id, 2, None, ALU.arith_shift_right))
            link(V.tensor_scalar(vti[:, :, 1], tok_id, 3, None, ALU.bitwise_and))
            ts(vt[:, :, 1], vti[:, :, 1], 2.0, ALU.mult, 1.0, ALU.add)
            link(V.tensor_copy(vt[:, :, 0], vti[:, :, 0]))
            link(V.tensor_copy(vtok[:, :, :, 0], vt[:, :, 0:1].to_broadcast([P, 5, NE])))
            tt(vtok[:, :, :, 1], m2, vt[:, :, 1:2].to_broadcast([P, 5, NE]), ALU.add)
            n = job("pos")
            wait_full(dve, n)
            link(V.tensor_reduce(cnt[:, 0:1], bank(n)[:, 5 * NE:6 * NE], AX_X, ALU.max))
            done(V.scalar_tensor_tensor(out=posm, in0=bank(n)[:, 0:5 * NE].rearrange("p (i e) -> p i e", e=NE), scalar=1.0,
                                        in1=mask, op0=ALU.add, op1=ALU.mult))
            ts(posm, posm, -1.0, ALU.add)
            ts(cnt[:, 1:2], cnt[:, 0:1], float(P), ALU.is_gt, 1.0, ALU.add)
            for r in range(2, RANKS):
                out = npass if r == RANKS - 1 else cnt[:, 1:2]
                stt(out, cnt[:, 0:1], float(P * r), cnt[:, 1:2], ALU.is_gt, ALU.add)
            dve.sem_inc(route_ready, 1)

            passes = dve.value_load(npass[0:1, 0:1], min_val=1, max_val=RANKS)

            def step_link(ins, s, value):
                ins.then_inc(s, 1)
                dve.wait_ge(s, value)

            def one_hot(p, k, n):
                if not (isinstance(k, int) and k < 2):
                    dve.wait_ge(idx_done, p * NE + k - 1)
                src = posm[:, :, k:k + 1] if isinstance(k, int) else posm[:, :, bass.ds(k, 1)]
                V.tensor_tensor(onehot[n % 2], iota.unsqueeze(1).to_broadcast([P, 5, P]),
                                src.to_broadcast([P, 5, P]), ALU.is_equal).then_inc(oh_ready, 1)

            def indices(p, k, n):
                dve.wait_ge(idx_done, p * NE + k + 1)
                base = (p * NE + k) * 4
                ps_ = banks[5][:, 0:2]
                step_link(V.tensor_scalar(idxf[:, 0:1], ps_[:, 0:1], 8.0, None, ALU.mult), idx_step, base + 1)
                step_link(V.tensor_tensor(idxf[:, 1:2], idxf[:, 0:1], ps_[:, 1:2], ALU.add), idx_step, base + 2)
                step_link(V.tensor_scalar(idxf[:, 2:3], idxf[:, 1:2], 0.0, OOB - 1.0, ALU.is_equal, ALU.mult), idx_step, base + 3)
                step_link(V.scalar_tensor_tensor(out=idx[:, n % 4, 0:1], in0=idxf[:, 1:2], scalar=-1.0, in1=idxf[:, 2:3],
                                                 op0=ALU.add, op1=ALU.add), idx_step, base + 4)
                V.tensor_scalar(idx[:, n % 4, 1:2], idx[:, n % 4, 0:1], 1, None, ALU.arith_shift_right).then_inc(idx_ready, 1)

            def gate_up(p, k, n):
                dve.wait_ge(gs_ready, p * NE + k + 1)
                if not (isinstance(k, int) and k < 2):
                    dve.wait_ge(heT_done, p * NE + k - 1)
                V.tensor_tensor(he[n % 2], gate_s[n % 2], banks[2 + n % 2][:, DE:2 * DE], ALU.mult).then_inc(he_ready, 1)

            def y_evac(p, k, n):
                dve.wait_ge(down_done, p * NE + k + 1)
                if not (isinstance(k, int) and k < 2):
                    dve.wait_ge(scattered[n % 2], p * (8 * NE) + used(k, n))
                V.tensor_copy(yo[n % 2][:, 0:512], banks[6][:, :])
                V.tensor_copy(yo[n % 2][:, 512:1024], banks[7][:, :]).then_inc(yo_ready, 1)

            def used(k, n):
                if isinstance(k, int):
                    return 16 * (k // 2)
                return (k - n % 2) * 8

            def step(p, k, n, first=False, ahead=True):
                if ahead:
                    one_hot(p, k + 2, n + 2)
                gate_up(p, k, n)
                if not first:
                    y_evac(p, k - 1, n - 1)
                if ahead:
                    indices(p, k + 2, n + 2)

            dve.sem_inc(pass_open, 1)
            with dve.Fori(0, passes) as p:
                for n in range(2):
                    one_hot(p, n, n)
                    indices(p, n, n)
                for n in range(4):
                    step(p, n, n, first=(n == 0))
                with dve.Fori(1, NE // 4 - 1) as g:
                    for n in range(4):
                        step(p, g * 4 + n, n)
                for n in range(NE - 4, NE):
                    step(p, n, n, ahead=(n < NE - 2))
                y_evac(p, NE - 1, NE - 1)
                for b in range(2):
                    dve.wait_ge(scattered[b], p * (8 * NE) + 8 * NE)
                V.tensor_scalar(iota, iota, float(P), None, ALU.add).then_inc(pass_open, 1)
                dve.wait_ge(pass_open, p + 2)

            def add_up(i):
                rows = TILES[i][1]
                gt = (gates if i < 4 else gates_s)[0:rows, 3, :]
                dve.wait_ge(y_in[i % 2], 16 * (i // 2 + 1))
                a_ = acc[i % 2][0:rows, :]
                ts(a_, y01[i % 2][0:rows, 0, :], wk[0:rows, i, 0:1], ALU.mult)
                stt(a_, y01[i % 2][0:rows, 1, :], wk[0:rows, i, 1:2], a_, ALU.mult, ALU.add)
                tt(a_, a_, gt, ALU.mult)
                V.tensor_tensor(x1[0:rows, i, :], x1[0:rows, i, :], a_, ALU.add).then_inc(acc_ready, 1)

            def finish(i):
                rows = TILES[i][1]
                dve.wait_ge(rstd2_ready, i + 1)
                if i >= 2:
                    dve.wait_ge(y_out[i % 2], 16 * (i // 2))
                V.scalar_tensor_tensor(out=x2[i % 2][0:rows, :], in0=x1[0:rows, i, :], scalar=rstd[0:rows, i:i + 1],
                                       in1=fg[0:rows, :], op0=ALU.mult, op1=ALU.mult).then_inc(y_ready, 1)

            for i in range(6):
                if i < 5:
                    add_up(i)
                if i > 0:
                    finish(i - 1)

        @block.tensor
        def _(pe):
            mm = nc.tensor.matmul

            def fill(n, ins):
                ins.then_inc(bank_full, 1)

            def open_job(name, key=0):
                n = job(name, key)
                assert n == open_job.next
                open_job.next += 1
                if n >= 8:
                    wait_emptied(pe, n - 8)
                return n, bank(n)
            open_job.next = 0

            def block_at(kind, c=0):
                n = BLOCK_OF[(kind, c)]
                pe.wait_ge(block_in[n % NBUF], block_value(n))
                return block_buf[n % NBUF]

            def ada(c):
                w = block_at("ada", c)
                n, bk = open_job("ada", c)
                for k in range(KT):
                    ins = mm(bk[0:ROWS, :], silT[:, k, :], w[:, k, :], start=(k == 0), stop=(k == KT - 1))
                fill(n, ins)

            def project(c, name):
                w = block_at("in", c)
                for f in range(FT):
                    n, bk = open_job(name, f)
                    for k in range(KT):
                        ins = mm(bk[:, :], w[:, k, P * f:P * (f + 1)], hT[:, k, 0:NP_TOK], start=(k == 0), stop=(k == KT - 1))
                    fill(n, ins)
                n, bk = open_job(name + "s")
                for f in range(FT):
                    for k in range(KT):
                        ins = mm(bk[:, NS_TOK * f:NS_TOK * (f + 1)], w[:, k, P * f:P * (f + 1)], hT[:, k, NP_TOK:TOK],
                                 start=(k == 0), stop=(k == KT - 1))
                fill(n, ins)

            pe.wait_ge(sil_ready, 1)
            for c in range(4):
                ada(c)
            pe.wait_ge(consts, 1)
            pe.wait_ge(mod_row_ready, 4)
            n, bk = open_job("modT")
            for m in range(2 * KT):
                ins = nc.tensor.transpose(bk[:, ROWS * m:ROWS * (m + 1)], mod_row[:, P * m:P * (m + 1)], ident[0:ROWS, 0:ROWS])
            fill(n, ins)
            for i in range(4):
                pe.wait_ge(xn_ready, i + 1)
                for h in range(2):
                    n, bk = open_job("xT", (i, h))
                    for k in range(4):
                        ins = nc.tensor.transpose(bk[:, P * k:P * (k + 1)], x_tok[:, i, P * (4 * h + k):P * (4 * h + k + 1)], ident)
                    fill(n, ins)
            pe.wait_ge(xn_ready, 5)
            n, bk = open_job("xTs")
            for k in range(KT):
                ins = nc.tensor.transpose(bk[:, NS_TOK * k:NS_TOK * (k + 1)], x_tok[0:NS_TOK, 4, P * k:P * (k + 1)],
                                          ident[0:NS_TOK, 0:NS_TOK])
            fill(n, ins)
            wait_emptied(pe, job("xT", (3, 0)))
            pe.wait_ge(hs_ready, 1)
            project(0, "zu")
            pe.wait_ge(w_ready, 1)
            for r in range(2):
                for q in range(4):
                    n, bk = open_job("WT", (r, q))
                    for j in range(4):
                        ins = nc.tensor.transpose(bk[:, P * j:P * (j + 1)],
                                                  w_p[r][:, 4 * q + j].rearrange("p l h -> p (l h)"), ident)
                    fill(n, ins)
            pe.wait_ge(ca_ready, 1)
            for q in range(4):
                for e in range(2):
                    n, bk = open_job("G", (e, q))
                    half_p = slice(ST * e, ST * (e + 1))
                    for j in range(4):
                        for r in range(2):
                            ins = mm(bk[0:GH, P * j:P * (j + 1)], bb[r][half_p, 4 * q + j, :],
                                     CA[r][half_p, 4 * q + j, 0:CH, :].rearrange("p d h -> p (d h)"),
                                     start=(r == 0), stop=(r == 1))
                    fill(n, ins)
            wait_emptied(pe, job("zus"))
            for f in range(FT):
                for h in range(2):
                    n, bk = open_job("U1", (f, h))
                    for l in range(4):
                        ins = nc.tensor.transpose(bk[0:UC, P * l:P * (l + 1)], u_ph[:, f, 4 * h + l, :], ident)
                    fill(n, ins)
            wait_emptied(pe, job("U1", (3, 0)))
            wait_emptied(pe, job("U1", (3, 1)))
            for q in range(8):
                n, bk = open_job("U2", q)
                for g in range(4):
                    ins = nc.tensor.transpose(bk[:, UC * g:UC * (g + 1)], u_cm[:, 4 * q + g].rearrange("p l h -> p (l h)"),
                                              ident[0:UC, 0:UC])
                fill(n, ins)
            wait_emptied(pe, job("U2", 6))
            wait_emptied(pe, job("U2", 7))
            for q in range(4):
                for r in range(2):
                    n, bk = open_job("S", (r, q))
                    for j in range(4):
                        for e in range(2):
                            ins = mm(bk[ST * e:ST * (e + 1), UC * j:UC * (j + 1)], WT[r][:, 4 * q + j, ST * e:ST * (e + 1)],
                                     u_pk[:, 2 * (4 * q + j) + e, :], start=True, stop=True)
                    fill(n, ins)
            project(1, "zc")
            project(2, "zv")
            project(3, "zb")
            for c in range(4, 12):
                ada(c)
            pe.wait_ge(scan_done, 1)
            pe.wait_ge(T_built, 16 * CH)
            for q in range(4):
                for e in range(2):
                    n, bk = open_job("Y", (q, e))
                    half_p = slice(ST * e, ST * (e + 1))
                    for j in range(4):
                        jj = 4 * q + j
                        out = bk[0:YC, P * j:P * (j + 1)]
                        mm(out, u_pk[:, 2 * jj + e, 0:YC], T[:, 2 * jj + e, :], start=True, stop=False)
                        for r in range(2):
                            ins = mm(out, X[r][half_p, jj, 0:YC],
                                     CA[r][half_p, jj, 1:CH + 1, :].rearrange("p d h -> p (d h)"),
                                     start=False, stop=(r == 1))
                    fill(n, ins)
            wait_emptied(pe, job("Y", (3, 1)))
            for f in range(FT):
                for h in range(2):
                    n, bk = open_job("YT", (f, h))
                    for l in range(4):
                        ins = nc.tensor.transpose(bk[:, YC * l:YC * (l + 1)], y_cm[:, 4 * h + l, 8 * f:8 * f + 8, :].rearrange("p g h -> p (g h)"),
                                                  ident[0:YC, 0:YC])
                    fill(n, ins)
            w = block_at("glu")
            for m in range(FT):
                n, bk = open_job("gl", m)
                for k in range(FT):
                    pe.wait_ge(gelu_done, k + 1)
                    ins = mm(bk[:, :], w[:, k, P * m:P * (m + 1)], yT[:, k, 0:NP_TOK], start=(k == 0), stop=(k == FT - 1))
                fill(n, ins)
            n, bk = open_job("gls")
            for m in range(FT):
                for k in range(FT):
                    ins = mm(bk[:, NS_TOK * m:NS_TOK * (m + 1)], w[:, k, P * m:P * (m + 1)], yT[:, k, NP_TOK:TOK],
                             start=(k == 0), stop=(k == FT - 1))
            fill(n, ins)
            n, bk = open_job("ss")
            pe.wait_ge(consts, 2)
            for which, src, ready in ((0, sqc, sqc_ready), (1, sq, sq_ready)):
                pe.wait_ge(ready, 1)
                for i, (t0, rows) in enumerate(TILES):
                    for k in range(FT):
                        ins = mm(bk[0:rows, 5 * which + i:5 * which + i + 1], src[:, k, t0:t0 + rows], one,
                                 start=(k == 0), stop=(k == FT - 1))
            fill(n, ins)
            pe.wait_ge(ymix_ready, 1)
            wo = [block_at("out", c) for c in range(2)]
            for i in range(6):
                if i < 5:
                    t0, rows = TILES[i]
                    for h in range(2):
                        for name, src, k0 in (("mc", y_conv, 0), ("ms", sg, FT)):
                            n, bk = open_job(name, (i, h))
                            for k in range(FT):
                                ins = mm(bk[0:rows, :], src[:, k, t0:t0 + rows], wo[h][:, k0 + k, :],
                                         start=(k == 0), stop=(k == FT - 1))
                            fill(n, ins)
                if i > 0:
                    rows = TILES[i - 1][1]
                    pe.wait_ge(h2_ready, i)
                    for h in range(2):
                        n, bk = open_job("hT", (i - 1, h))
                        for k in range(4):
                            kk = 4 * h + k
                            ins = nc.tensor.transpose(bk[:, P * k:P * k + rows], h2[(i - 1) % 2][0:rows, P * kk:P * (kk + 1)],
                                                      ident[0:rows, 0:rows])
                        fill(n, ins)
                    n, bk = open_job("rl", i - 1)
                    wait_emptied(pe, job("hT", (i - 1, 1)))
                    pe.wait_ge(wr_in, 32)
                    for k in range(KT):
                        ins = mm(bk[0:rows, 0:NG + NE], h2T[(i - 1) % 2][:, k, 0:rows], wr[:, k, :],
                                 start=(k == 0), stop=(k == KT - 1))
                    fill(n, ins)
            pe.wait_ge(mask_ready, 1)
            n, bk = open_job("pos")
            for i in range(6):
                out = bk[:, NE * i:NE * (i + 1)]
                for j in range(min(i, 4) + 1):
                    own = j == i
                    ins = mm(out, tri if own else ones_b, mask_b[:, j, :], start=(j == 0), stop=(j == min(i, 4)))
            fill(n, ins)
            wait_emptied(pe, job("pos"))
            wait_emptied(pe, job("hT", (4, 1)))

            pe.wait_ge(route_ready, 1)
            passes = pe.value_load(npass[0:1, 0:1], min_val=1, max_val=RANKS)

            def find(p, k, n):
                pe.wait_ge(oh_ready, p * NE + k + 1)
                after(pe, idx_ready, p, k)
                for i in range(5):
                    v = vtok[:, i, k, :] if isinstance(k, int) else vtok[:, i, bass.ds(k, 1), :].rearrange("p o v -> p (o v)")
                    ins = mm(banks[5][:, 0:2], onehot[n % 2][:, i, :], v, start=(i == 0), stop=(i == 4))
                ins.then_inc(idx_done, 1)

            def turn(p, k, n):
                pe.wait_ge(gathered[n % 2], p * (8 * NE) + (16 * (k // 2 + 1) if isinstance(k, int) else (k - n % 2) * 8 + 16))
                after(pe, xgT_ready, p, k)
                for h in range(KT):
                    ins = nc.tensor.transpose(banks[h // 4][:, P * (h % 4):P * (h % 4 + 1)], xg[n % 2][:, P * h:P * (h + 1)], ident)
                ins.then_inc(tr_done, 1)

            def gate_up(p, k, n):
                s = (n + 3) % NSLOT
                pe.wait_ge(slot_full[s], p * (4 * NE) + (16 * (k // 4 + 1) if isinstance(k, int) else (k - n % 4) * 4 + 16))
                pe.wait_ge(xgT_ready, p * NE + k + 1)
                if not (isinstance(k, int) and k < 2):
                    pe.wait_ge(he_ready, p * NE + k - 1)
                for h in range(KT):
                    ins = mm(banks[2 + n % 2][:, :], xgT[n % 2][:, h, :], slot_in[s][:, h, :], start=(h == 0), stop=(h == KT - 1))
                ins.then_inc(gu_done, 1)

            def turn_he(p, k, n):
                pe.wait_ge(he_ready, p * NE + k + 1)
                after(pe, heT_ready, p, k)
                for h in range(2):
                    ins = nc.tensor.transpose(banks[4][:, P * h:P * (h + 1)], he[n % 2][:, P * h:P * (h + 1)], ident)
                ins.then_inc(heT_done, 1)

            def down(p, k, n):
                s = (n + 3) % NSLOT
                pe.wait_ge(heT_ready, p * NE + k + 1)
                after(pe, yo_ready, p, k)
                for c in range(2):
                    for h in range(2):
                        ins = mm(banks[6 + c][:, :], heT[:, h, :], slot_down[s][:, h, 512 * c:512 * c + 512],
                                 start=(h == 0), stop=(h == 1))
                ins.then_inc(down_done, 1)

            def step(p, k, n, first=False, turn_next=True, find_next=True):
                if not first:
                    turn_he(p, k - 1, n - 1)
                gate_up(p, k, n)
                if not first:
                    down(p, k - 1, n - 1)
                if turn_next:
                    turn(p, k + 1, n + 1)
                if find_next:
                    find(p, k + 2, n + 2)

            with pe.Fori(0, passes) as p:
                pe.wait_ge(pass_open, p + 1)
                for n in range(2):
                    find(p, n, n)
                turn(p, 0, 0)
                for n in range(4):
                    step(p, n, n, first=(n == 0))
                with pe.Fori(1, NE // 4 - 1) as g:
                    for n in range(4):
                        step(p, g * 4 + n, n)
                for n in range(NE - 4, NE):
                    step(p, n, n, turn_next=(n < NE - 1), find_next=(n < NE - 2))
                turn_he(p, NE - 1, NE - 1)
                down(p, NE - 1, NE - 1)


OUTS = {"y_prompt": (NP_TOK, D), "y_sample": (NS_TOK, D), "o_conv_p": (P, FT, 2), "o_conv_s": (P, FT, NB, 2),
        "o_ssm_p": (P, 2 * NJ), "o_ssm_s": (P, 2 * NJ * NB)}


def kernel(**inputs):
    import numpy as np
    import concourse.bacc as _bacc
    from concourse import mybir as _mybir
    from concourse.bass_utils import run_bass_kernel_spmd as _run

    x = {k: np.asarray(v) for k, v in inputs.items()}

    def states(a):
        a = a.reshape((NJ, 2, ST) + a.shape[2:])
        return np.moveaxis(a, 0, 2).reshape((P, NJ) + a.shape[3:])

    def feats(a):
        return np.moveaxis(a.reshape(a.shape[:-1] + (FT, P)), (-1, -2), (0, 1))

    def blocks(w, n):
        k = w.shape[0] // P
        return w.reshape(k, P, n, 512).transpose(2, 1, 0, 3).reshape(n, P, k * 512)

    w_in = x["w_in"][0].reshape(D, 4, 512)[:, [3, 1, 2, 0], :].reshape(D, 4 * 512)
    c = np.concatenate([x["c_prompt"], x["c_sample"]], 0)
    gate_up = np.concatenate([x["w_expert_gate"][0], x["w_expert_up"][0]], 2)
    gate_up = gate_up.reshape(NE, KT, P, 2 * DE).transpose(0, 2, 1, 3).reshape(NE, P, KT * 2 * DE)
    down = x["w_expert_down"][0].reshape(NE, 2, P, D).transpose(0, 2, 1, 3).reshape(NE, P, 2 * D)
    router = np.concatenate([x["w_router_group"][0], x["w_router_expert"][0].transpose(1, 0, 2).reshape(D, NE)], 1)
    b_router = np.concatenate([x["b_router_group"][0], x["b_router_expert"][0].reshape(NE)])
    vectors = [x["ssm_d"][0], x["b_glu"][0], x["out_norm_conv_g"][0], x["out_norm_ssm_g"][0], *x["conv_w"][0]]
    arrays = {
        "x_prompt": x["x_prompt"][0], "x_sample": x["x_sample"].reshape(NS_TOK, D),
        "cT": c.reshape(ROWS, KT, P).transpose(2, 1, 0),
        "w_ada": blocks(x["w_ada"][0], 12), "w_in": blocks(w_in, 4), "w_out": blocks(x["w_out"][0], 2),
        "w_glu": blocks(x["w_glu"][0], 1)[0], "w_exp": np.concatenate([gate_up, down], 2),
        "b_ada": np.broadcast_to(x["b_ada"][0], (ROWS, 6 * D)),
        "g1": np.broadcast_to(x["norm1_g"][0], (ROWS, D)), "g2": np.broadcast_to(x["norm2_g"][0], (ROWS, D)),
        "final_g": np.broadcast_to(x["final_norm_g"], (P, D)),
        "w_router": router.reshape(KT, P, NG + NE).transpose(1, 0, 2), "b_router": np.broadcast_to(b_router, (P, NG + NE)),
        "lam": np.stack([states(x["lambda_re"][0]), states(x["lambda_im"][0]),
                         states(np.broadcast_to(x["log_dt"][0][:, None], (GR, ST)))], 1),
        "bc": np.stack([states(x["ssm_b_re"][0]).reshape(P, -1), states(x["ssm_b_im"][0]).reshape(P, -1),
                        states(x["ssm_c_re"][0].transpose(0, 2, 1)).reshape(P, -1),
                        states(x["ssm_c_im"][0].transpose(0, 2, 1)).reshape(P, -1)], 1),
        "fvec": np.stack([feats(v) for v in vectors], 2),
        "conv_state": feats(x["state_conv"][0]),
        "h0": np.stack([states(x[k][0].transpose(1, 2, 0)) for k in ("state_ssm_re", "state_ssm_im")], 0),
    }
    arrays = {k: np.ascontiguousarray(v) for k, v in arrays.items()}
    nc = _bacc.Bacc("TRN2", target_bir_lowering=False, num_devices=1)
    t = {}
    for name, a in arrays.items():
        t[name] = nc.dram_tensor(f"in_{name}", a.shape, _mybir.dt.from_np(a.dtype), kind="ExternalInput").ap()
    for name, shape in OUTS.items():
        t[name] = nc.dram_tensor(f"out_{name}", shape, _mybir.dt.float32, kind="ExternalOutput").ap()
    build(nc, t)
    r = _run(nc, [{f"in_{k}": a for k, a in arrays.items()}], core_ids=[0]).results[0]
    o = {k: np.asarray(r[f"out_{k}"]) for k in OUTS}

    def groups(a):
        a = a.reshape((2, ST, NJ) + a.shape[2:])
        a = np.moveaxis(a, (2, 0, 1), (-3, -2, -1))
        return a.reshape(a.shape[:-3] + (GR, ST))

    conv_p = o["o_conv_p"].transpose(2, 1, 0).reshape(1, 1, 2, FT * P)
    conv_s = o["o_conv_s"].transpose(2, 3, 1, 0).reshape(1, NB, 2, FT * P)
    ssm_p = o["o_ssm_p"].reshape(P, 2, NJ)
    ssm_s = o["o_ssm_s"].reshape(P, 2, NJ, NB)
    return (o["y_prompt"].reshape(1, NP_TOK, D), o["y_sample"].reshape(NB, NS, D), conv_p,
            groups(ssm_p[:, 0]).reshape(1, 1, GR, ST), groups(ssm_p[:, 1]).reshape(1, 1, GR, ST),
            conv_s, groups(ssm_s[:, 0]).reshape(1, NB, GR, ST), groups(ssm_s[:, 1]).reshape(1, NB, GR, ST))
```

```python
from contextlib import ExitStack
import math

import concourse.bass as bass
from concourse import mybir

F32 = mybir.dt.float32
F32R = mybir.dt.float32r
BF16 = mybir.dt.bfloat16
I32 = mybir.dt.int32
ALU = mybir.AluOpType
ACT = mybir.ActivationFunctionType
AX_X = mybir.AxisListType.X

P = 128
D = 1024
KT = D // P
NP_TOK, NB, NS = 512, 8, 4
NS_TOK = NB * NS
TOK = NP_TOK + NS_TOK
TILES = [(0, 128), (128, 128), (256, 128), (384, 128), (512, 32)]
ROWS = 1 + NB
FT = 4
CH = 8
NC = NP_TOK // CH
YC = NB + NC
UC = YC + NB
GR, GH, ST = 32, 16, 64
NJ = GR // 2
NG, NE_G = 4, 8
NE = NG * NE_G
DE = 256
CAP = 64
RANKS = -(-TOK // CAP)
EPS = 1e-6
BIG = 1.0e30
CHUNK = KT * 512
EXPERT = KT * 2 * DE + 2 * D
NBUF = 3
NSLOT = 3
BODY = 6
HEAD = 4
SPAN = (NE - HEAD) // BODY
OOB = 4096.0


def KB(k):
    return int(256 * k)


STREAM = ([("ada", c) for c in range(4)] + [("in", c) for c in range(4)]
          + [("ada", c) for c in range(4, 12)] + [("glu", 0), ("out", 0), ("out", 1)])
BLOCK_OF = {name: n for n, name in enumerate(STREAM)}


def bank_jobs():
    jobs = [("ada", c, "v") for c in range(4)] + [("modT", 0, "v")]
    for i in range(4):
        jobs += [("xT", (i, 0), "a"), ("xT", (i, 1), "v")]
    jobs += [("xTs", 0, "v")]
    jobs += [("zu", f, "a") for f in range(FT)] + [("zus", 0, "a")]
    jobs += [("WT", (r, q), "a") for r in range(2) for q in range(4)]
    jobs += [("U1", (f, h), "a") for f in range(FT) for h in range(2)]
    jobs += [("G", (e, q), "a") for q in range(4) for e in range(2)]
    jobs += [("U2", q, "av"[q % 2]) for q in range(8)]
    jobs += [("S", (r, q), "v") for q in range(4) for r in range(2)]
    jobs += [("zc", f, "a") for f in range(FT)] + [("zcs", 0, "a")]
    jobs += [("zv", f, "v") for f in range(FT)] + [("zvs", 0, "v")]
    jobs += [("zb", f, "v") for f in range(FT)] + [("zbs", 0, "v")]
    jobs += [("ada", c, "v") for c in range(4, 12)]
    jobs += [("Y", (q, e), "a") for q in range(4) for e in range(2)]
    jobs += [("YT", (f, h), "v") for f in range(FT) for h in range(2)]
    jobs += [("ss", 0, "v")]
    jobs += [("gl", m, "a") for m in range(FT)] + [("gls", 0, "a")]
    jobs += [("mc", (0, 0), "a"), ("mc", (0, 1), "a"), ("mc", (1, 0), "a"), ("ss", 1, "v")]
    for i in range(6):
        if i < 5:
            jobs += [("ms", (i, 0), "v")]
        if i > 0:
            jobs += [("hT", (i - 1, 0), "a"), ("hT", (i - 1, 1), "a")]
        if i < 4:
            jobs += [("mc", (i + 1, 1), "a")]
        if i < 5:
            jobs += [("ms", (i, 1), "v")]
        if i < 3:
            jobs += [("mc", (i + 2, 0), "a")]
        if i > 0:
            jobs += [("rl", i - 1, "v")]
    jobs += [("pos", 0, "v")]
    return jobs


JOBS = bank_jobs()
JOB_OF = {(name, key): n for n, (name, key, _) in enumerate(JOBS)}


def emptied(n):
    owner = JOBS[n][2]
    return owner, sum(o == owner for _, _, o in JOBS[:n + 1])


def build(nc, t):
    ctx = ExitStack()
    with ctx:
        def sem(name):
            return ctx.enter_context(nc.semaphore(name))

        arena_start = -(-nc.sbuf_base // 32) * 32
        arena = ctx.enter_context(nc.sbuf_tensor("arena", [P, KB(207.5)], F32))
        banks = [ctx.enter_context(nc.psum_tensor(f"bank{b}", [P, 512], F32)) for b in range(8)]

        def at(k, *shape, rows=P, dt=F32):
            n = 1
            for s in shape:
                n *= s
            words = n if dt != BF16 else (n + 1) // 2
            v = arena[0:rows, KB(k):KB(k) + words]
            if dt != F32:
                v = v.bitcast(dt)
            if len(shape) == 1:
                return v
            names = "abcd"[:len(shape)]
            return v.rearrange(f"p ({' '.join(names)}) -> p {' '.join(names)}",
                               **{names[i]: shape[i] for i in range(1, len(shape))})

        def rounded(name, k, words):
            return nc.alloc_sbuf_tensor_at(name, [P, words], F32R, offset=arena_start + 4 * KB(k))[:, :]

        def bc3(v, shape):
            for _ in range(len(shape) - v.ndim):
                v = v.unsqueeze(v.ndim)
            return v.to_broadcast(shape)

        block_buf = [at(16 * b, KT, 512) for b in range(NBUF)]
        SLOT_AT = (72, 48, 24)
        slot = [at(k, EXPERT) for k in SLOT_AT]
        PARTS = [(0, 4 * 512), (4 * 512, 8 * 512), (8 * 512, 8 * 512 + D), (8 * 512 + D, EXPERT)]
        raw = [[s[:, a:b] for a, b in PARTS] for s in slot]
        lo = [[rounded(f"lo{s}_{n}", SLOT_AT[s] + a / 256, b - a) for n, (a, b) in enumerate(PARTS)] for s in range(NSLOT)]
        hi = [[rounded(f"hi{h}_{n}", k, b - a) for n, (k, (a, b)) in enumerate(zip(ks, PARTS))]
              for h, ks in enumerate(((0, 8, 16, 20), (116, 133, 124, 141)))]
        w_p = [at(48, NJ, CH, GH), at(56, NJ, CH, GH)]
        u_cm = at(48, GR, CH, GH, rows=UC)
        rot_a, rot_b = at(48, NJ, NC), at(52, NJ, NC)
        rot_w = [at(56, NJ, NC), at(60, NJ, NC)]
        g2_row = at(48, D, rows=ROWS)
        mod_out = at(52, 2, 512, rows=ROWS)
        y_cm = at(48, CH, GR, GH, rows=YC)
        g1_row = at(64, D, rows=ROWS)
        X = [at(64, NJ, NB + 1 + NC), at(68.6875, NJ, NB + 1 + NC)]
        mix_t = [at(16 + 2 * n, 512) for n in range(4)]
        ada_bias = at(73.5, NBUF, 512, rows=ROWS)
        first_bias = at(121, 4 * 512, rows=ROWS)
        T = at(80, GR, CH * GH)
        x_tok = at(96, 5, D)
        g_sb = at(96, GR, CH * GH, rows=GH)
        y_conv = at(96, FT, TOK)
        cv_p = at(105, FT, 2 + NP_TOK)
        cv_s = at(113.125, FT, NB, 2 + NS)
        h2T = [at(105, KT, P), at(109, KT, P)]
        hT = at(116, KT, TOK)
        gates = at(116, 4, D)
        WT = [at(133, NJ, P), at(141, NJ, P)]
        gates_s = at(133, 4, D, rows=NS_TOK)
        CA = [at(149, NJ, CH + 1, GH), at(158, NJ, CH + 1, GH)]
        u_ph = at(167, FT, CH, UC)
        x1 = at(149, 5, D)
        fg = at(169, D)
        par = at(177, 2560)
        u_pk = at(177, GR, UC)
        sg = at(177, FT, TOK)
        mod_row = at(187, 2 * D, rows=ROWS)
        E = [at(187, NJ, NC), at(191, NJ, NC)]
        yT = at(187, FT, TOK)
        h2 = [at(187, D), at(191, D)]

        def tmp_at(*shape):
            return at(195, *shape)

        st_s, st_tmp = at(132, 2, NJ, NB), at(114, NJ, NB)
        junk_x, junk_m = at(116, D), at(195.5, D)
        w_tmp = at(200, NJ, GH)
        S = [at(195, NJ, UC), at(200, NJ, UC)]
        sq = at(195.5, FT, TOK)
        sqc = at(105, FT, TOK)
        ident = at(205, P)
        small = at(205.5, 512)
        fvec = small[:, 0:FT * 7].rearrange("p (f v) -> p f v", v=7)
        one = small[:, 28:29]
        modT = small[:, 32:32 + 2 * KT * ROWS].rearrange("p (m r) -> p m r", r=ROWS)
        cT = small[:, 176:176 + KT * ROWS].rearrange("p (k r) -> p k r", r=ROWS)
        silT = small[:, 248:248 + KT * ROWS].rearrange("p (k r) -> p k r", r=ROWS)
        a4 = [small[:, 320:336], small[:, 336:352]]
        r8 = small[:, 352:368]
        st_p = small[:, 432:464].rearrange("p (r j) -> p r j", r=2)
        ms = small[:, 384:389]
        rstd = small[:, 389:394]
        ms_m = small[:, 394:404]
        rstd_m = small[:, 404:414]
        half = small[:, 414:424]
        npass = small[:, 424:425].bitcast(I32)
        cnt = small[:, 425:430]
        off = [0]

        def par_at(*shape):
            n = math.prod(shape)
            v = par[:, off[0]:off[0] + n]
            off[0] += n
            if len(shape) > 1:
                ax = "abc"[:len(shape)]
                v = v.rearrange(f"p ({' '.join(ax)}) -> p {' '.join(ax)}",
                                **{ax[i]: shape[i] for i in range(1, len(shape))})
            return v

        lam = par_at(3, NJ)
        lr, li, ldt = lam[:, 0, :], lam[:, 1, :], lam[:, 2, :]
        bc = par_at(4, NJ * GH)
        b_in = [bc[:, r, :].rearrange("p (j h) -> p j h", h=GH) for r in range(2)]
        c_in = [bc[:, 2 + r, :].rearrange("p (j h) -> p j h", h=GH) for r in range(2)]
        bb = [par_at(NJ, GH), par_at(NJ, GH)]
        pw = [par_at(NJ, CH + 1), par_at(NJ, CH + 1)]
        dt_, k_, r_, ang, sin_h, den, am1, fr, fi = (par_at(NJ) for _ in range(9))
        x_, mag, sin_a, cos_a, *ph_ = (at(79.5 + n / 16, NJ) for n in range(8))
        ph = [ph_[0:2], ph_[2:4]]
        bits_ = par_at(NJ).bitcast(I32)
        assert off[0] <= 2560
        wr = at(114.5, KT, NG + NE)
        br = at(115.75, NG + NE)
        logit = at(173, 5, NG + NE)
        ex = at(173.75, 5, NG)
        gm = at(174, 5, 8)
        gone = at(174.25, 5, NG)
        les = at(175.25, 5, NE)
        m1 = at(176, 5, NE)
        m2 = at(96, 5, NE)
        mask = at(96.75, 5, NE)
        mask_b = at(97.5, 5, NE, dt=BF16)
        posm = at(98, 5, NE)
        tri = at(113, P, dt=BF16)
        ones_b = at(113.25, P, dt=BF16)
        iota = at(113.5, P)
        vtok = at(99.75, 5, NE, 2, dt=BF16)
        vt = at(114.1875, 5, 4)
        w32 = at(114, NE)
        w4 = at(114.125, NG)
        wk = at(101.5, 5, 2)
        vti = at(114.28125, 5, 2, dt=I32)
        tok_id = at(114.34375, 5, dt=I32)
        full_at = at(114.375, RANKS - 1)
        more = at(101, RANKS - 1)
        onehot = [at(102, 5, CAP, dt=BF16), at(103.25, 5, CAP, dt=BF16)]
        idx = at(104.5, BODY, 2, rows=CAP, dt=I32)
        idxf = at(104.75, 4, rows=CAP)
        xg = [at(105, D, rows=CAP), at(109, D, rows=CAP)]
        xh = [rounded("xh0", 181, KT * CAP), rounded("xh1", 183, KT * CAP)]
        xl = [rounded("xl0", 185, KT * CAP), rounded("xl1", 187, KT * CAP)]
        yo = [at(189, D, rows=CAP), at(193, D, rows=CAP)]
        gate_s = [at(197, DE, rows=CAP), at(198, DE, rows=CAP)]
        he = [at(199, DE, rows=CAP), at(200, DE, rows=CAP)]
        heh, hel = rounded("heh", 201, 2 * CAP), rounded("hel", 201.5, 2 * CAP)
        y01 = [at(0, 2, D), at(8, 2, D)]
        acc = [at(16, D), at(20, D)]
        x2 = [at(24, D), at(28, D)]
        junk = at(32, D)

        x_in = [sem(f"x_in{i}") for i in range(5)]
        c_loaded, row_in = sem("c_loaded"), sem("row_in")
        par_in, conv_in, g2_in, wr_in, x_again = (sem(n) for n in ("par_in", "conv_in", "g2_in", "wr_in", "x_again"))
        block_in = [sem(f"block_in{b}") for b in range(NBUF)]
        bias_in = [sem(f"bias_in{b}") for b in range(NBUF)]
        bank_full = sem("bank_full")
        bank_free = {"a": sem("bank_free_act"), "v": sem("bank_free_dve")}
        dchain, achain, pchain = sem("dve_chain"), sem("act_chain"), sem("pool_chain")
        consts, small_set = sem("consts"), sem("small_set")
        silu_e, sil_ready = sem("silu_exp"), sem("sil_ready")
        ss_x, rstd_ready, xn_ready = sem("ss_x"), sem("rstd_ready"), sem("xn_ready")
        ang_ready, sin_ready = sem("ang_ready"), sem("sin_ready")
        bbar_ready, w_ready, ca_ready = sem("bbar_ready"), sem("w_ready"), sem("ca_ready")
        T_zero, T_built = sem("T_zero"), sem("T_built")
        scan_done, states_ready, state_out = sem("scan_done"), sem("states_ready"), sem("state_out")
        cv_ready, conv_done = sem("cv_ready"), sem("conv_done")
        mod_row_ready = sem("mod_row_ready")
        mod_stored = [sem("mod_stored0"), sem("mod_stored1")]
        gates_in = sem("gates_in")
        yT_ready, gelu_done, ysm_ready = sem("yT_ready"), sem("gelu_done"), sem("ysm_ready")
        sqc_ready, sq_ready, ymix_ready = sem("sqc_ready"), sem("sq_ready"), sem("ymix_ready")
        yconv_ready = sem("yconv_ready")
        msm_ready, mrstd_ready = sem("msm_ready"), sem("mrstd_ready")
        mix_a, x1_ready = sem("mix_a"), sem("x1_ready")
        ss_x1, rstd1_ready, h2_ready = sem("ss_x1"), sem("rstd1_ready"), sem("h2_ready")
        h2_stored = [sem("h2_stored0"), sem("h2_stored1")]
        lg_ready, ex_ready, d_ready, dex_ready = sem("lg_ready"), sem("ex_ready"), sem("d_ready"), sem("dex_ready")
        moe_consts, mask_ready, route_ready = sem("moe_consts"), sem("mask_ready"), sem("route_ready")
        in_full = [sem(f"in_full{s}") for s in range(NSLOT)]
        down_full = [sem(f"down_full{s}") for s in range(NSLOT)]
        hi_in_ready, lo_in_ready = sem("hi_in_ready"), sem("lo_in_ready")
        hi_down_ready, lo_down_ready = sem("hi_down_ready"), sem("lo_down_ready")
        oh_ready, idx_done, idx_ready = sem("oh_ready"), sem("idx_done"), sem("idx_ready")
        gathered = [sem("gathered0"), sem("gathered1")]
        scattered = [sem("scattered0"), sem("scattered1")]
        rows_go = sem("rows_go")
        idx_step, h0_in, hs_ready = sem("idx_step"), sem("h0_in"), sem("hs_ready")
        tr_done, xh_ready, xl_ready = sem("tr_done"), sem("xh_ready"), sem("xl_ready")
        turn_go = sem("turn_go")
        gu_done, gs_ready, he_ready = sem("gu_done"), sem("gs_ready"), sem("he_ready")
        heT_done, heh_ready, hel_ready = sem("heT_done"), sem("heh_ready"), sem("hel_ready")
        down_done, yo_ready = sem("down_done"), sem("yo_ready")
        pass_open = sem("pass_open")
        y_in = [sem("y_in0"), sem("y_in1")]
        y1_ready = sem("y1_ready")
        acc_ready, ss_x2, rstd2_ready = sem("acc_ready"), sem("ss_x2"), sem("rstd2_ready")
        y_ready, y_out = sem("y_ready"), [sem("y_out0"), sem("y_out1")]

        mod_d = nc.dram_tensor("mod_rows", [ROWS, 4, D], F32, kind="Internal").ap()
        h2_d = nc.dram_tensor("h2_rows", [TOK, D], F32, kind="Internal").ap()
        y_d = nc.dram_tensor("expert_rows", [2 * TOK, D], F32, kind="Internal").ap()

        def job(name, key=0):
            return JOB_OF[(name, key)]

        def bank(n):
            return banks[n % 8]

        def wait_full(eng, n):
            eng.wait_ge(bank_full, n + 1)

        def wait_emptied(eng, n):
            owner, count = emptied(n)
            eng.wait_ge(bank_free[owner], count)

        def block_value(n):
            return 16 * (n // NBUF + 1)

        def last_job_of(n):
            kind, c = STREAM[n]
            if kind == "ada":
                return job("ada", c)
            if kind == "in":
                return job(("zus", "zcs", "zvs", "zbs")[c])
            return job("gls") if kind == "glu" else job("ms", (4, c))

        def number(g, c):
            return c if g is None else g * BODY + c

        def count(p, g, c, per=1, each=1):
            whole = each * (NE // per) * p + each * (c // per)
            return whole if g is None else whole + g * (each * (BODY // per))

        def arrived(p, g, c):
            uses = len(range(c % NSLOT, NE, NSLOT))
            value = p * (16 * uses) + 16 * (c // NSLOT + 1)
            return value if g is None else value + g * (16 * (BODY // NSLOT))

        block = ctx.enter_context(nc.Block())

        @block.sync
        def _(sp):
            sp.dma_start(cT, t["cT"]).then_inc(c_loaded, 16)
            for dst, src in ((lam, t["lam"]), (bc, t["bc"])):
                sp.dma_start(dst, src).then_inc(par_in, 16)
            for n, (kind, c) in enumerate(STREAM):
                b = n % NBUF
                if n == 1:
                    for dst, src in ((fvec, t["fvec"]), (g1_row, t["g1"]), (first_bias, t["b_ada"][:, 0:4 * 512])):
                        sp.dma_start(dst, src).then_inc(row_in, 16)
                if n == NBUF:
                    for i, (t0, rows) in enumerate(TILES):
                        src = t["x_prompt"][t0:t0 + rows, :] if i < 4 else t["x_sample"]
                        sp.dma_start(x_tok[0:rows, i, :], src).then_inc(x_in[i], 16)
                if kind == "ada" and c >= 4:
                    if c >= 4 + NBUF:
                        wait_emptied(sp, job("ada", c - NBUF))
                    sp.dma_start(ada_bias[:, c % NBUF, :], t["b_ada"][:, 512 * c:512 * c + 512]).then_inc(bias_in[c % NBUF], 16)
                if n >= NBUF:
                    wait_full(sp, last_job_of(n - NBUF))
                kts = FT if kind == "glu" else KT
                src = t["w_glu"] if kind == "glu" else t["w_" + kind][c]
                sp.dma_start(block_buf[b][:, 0:kts, :], src.rearrange("p (k n) -> p k n", k=kts)).then_inc(block_in[b], 16)

            def load(s, e):
                src = t["w_exp"][e] if isinstance(e, int) else t["w_exp"][bass.ds(e, 1)].rearrange("e p n -> (e p) n")
                return ((slot[s][:, 0:KT * 512], src[:, 0:KT * 512], in_full[s], gu_done),
                        (slot[s][:, KT * 512:EXPERT], src[:, KT * 512:EXPERT], down_full[s], down_done))

            def load_first(s):
                for dst, src, full, _ in load(s, s):
                    sp.dma_start(dst, src).then_inc(full, 16)

            def load_next(p, g, c):
                k = c if g is None else g * NSLOT + c
                for dst, src, full, used in load(c % NSLOT, k):
                    sp.wait_ge(used, p * NE + (c - NSLOT + 1) + (0 if g is None else g * NSLOT))
                    sp.dma_start(dst, src).then_inc(full, 16)

            def load_rest(p):
                with sp.Fori(0, NE // NSLOT - 1) as g:
                    for c in range(NSLOT, 2 * NSLOT):
                        load_next(p, g, c)
                for c in range(NE - NE % NSLOT, NE):
                    load_next(p, None, c)

            wait_full(sp, job("Y", (3, 1)))
            sp.wait_ge(states_ready, 1)
            load_first(0)
            wait_full(sp, job("YT", (3, 1)))
            load_first(1)
            sp.wait_ge(x1_ready, 10)
            load_first(2)
            load_rest(0)
            sp.wait_ge(route_ready, 1)
            passes = sp.value_load(npass[0:1, 0:1], min_val=1, max_val=RANKS)
            with sp.If(passes > 1):
                with sp.Fori(1, passes) as p:
                    sp.wait_ge(pass_open, p + 1)
                    for s in range(NSLOT):
                        load_first(s)
                    load_rest(p)

            def store_y(i):
                t0, n = TILES[i]
                sp.wait_ge(y_ready, i + 1)
                dst = t["y_prompt"][t0:t0 + n, :] if i < 4 else t["y_sample"]
                sp.dma_start(dst, x2[i % 2][0:n, :]).then_inc(y_out[i % 2], 16)

            sp.wait_ge(pass_open, passes + 1)
            for i, (t0, n) in enumerate(TILES):
                if i >= 2:
                    sp.wait_ge(acc_ready, i - 1)
                sp.dma_start(y01[i % 2][0:n], y_d[2 * t0:2 * (t0 + n), :].rearrange("(t k) d -> t k d", k=2)).then_inc(y_in[i % 2], 16)
                if i >= 2:
                    store_y(i - 2)
            store_y(3)
            store_y(4)
            sp.wait_ge(y_out[0], 16 * 3)
            sp.wait_ge(y_out[1], 16 * 2)

        @block.gpsimd
        def _(pool):
            def link(ins):
                link.n += 1
                ins.then_inc(pchain, 1)
                pool.wait_ge(pchain, link.n)
            link.n = 0

            def power(out, sums, tmp_, width, done):
                link(pool.tensor_scalar(tmp_, sums, 1.0 / width, EPS, ALU.mult, ALU.add))
                pool.tensor_tensor(out, tmp_, half[0:out.shape[0], 0:out.shape[1]], ALU.pow).then_inc(done, 1)

            link(pool.memset(ident, 0.0))
            pool.affine_select(out=ident, in_=ident, compare_op=ALU.not_equal, fill=1.0, base=0,
                               pattern=[[-1, P]], channel_multiplier=1).then_inc(consts, 1)
            pool.memset(one, 1.0).then_inc(consts, 1)
            pool.memset(small[:, 384:414], 1.0).then_inc(small_set, 1)
            link(pool.memset(half, -0.5))
            pool.memset(u_ph, 0.0).then_inc(consts, 1)
            pool.memset(T, 0.0).then_inc(T_zero, 1)
            pool.wait_ge(ss_x, 5)
            power(rstd, ms, rstd, D, rstd_ready)
            pool.wait_ge(bbar_ready, 1)
            for l in range(4, CH):
                al = [bc3(pw[r][:, :, CH - 1 - l], [P, NJ, GH]) for r in range(2)]
                o = [w_p[r][:, :, l, :] for r in range(2)]
                for r, op in ((0, ALU.subtract), (1, ALU.add)):
                    link(pool.tensor_tensor(o[r], al[0], bb[r], ALU.mult))
                    link(pool.tensor_tensor(w_tmp, al[1], bb[1 - r], ALU.mult))
                    link(pool.tensor_tensor(o[r], o[r], w_tmp, op))
            pool.sem_inc(w_ready, 1)
            for d in range(6, CH + 1):
                ad = [bc3(pw[r][:, :, d], [P, NJ, GH]) for r in range(2)]
                o = [CA[r][:, :, d, :] for r in range(2)]
                for r, op in ((0, ALU.subtract), (1, ALU.add)):
                    link(pool.tensor_tensor(o[r], ad[0], c_in[r], ALU.mult))
                    link(pool.tensor_tensor(w_tmp, ad[1], c_in[1 - r], ALU.mult))
                    link(pool.tensor_tensor(o[r], o[r], w_tmp, op))
                link(pool.tensor_scalar(o[1], o[1], -1.0, None, ALU.mult))
            pool.sem_inc(ca_ready, 1)
            wait_emptied(pool, job("xTs"))
            pool.dma_start(cv_s[:, :, :, 0:2], t["conv_state"]).then_inc(conv_in, 16)
            for r in range(2):
                pool.dma_start(X[r][:, :, 0:NB], t["h0"][r]).then_inc(h0_in, 16)
            pool.wait_ge(T_zero, 1)
            wait_emptied(pool, job("G", (1, 3)))
            for l in range(CH):
                pool.dma_start(T[GH * l:GH * (l + 1), :, GH * l:CH * GH],
                               g_sb[:, :, 0:(CH - l) * GH]).then_inc(T_built, 16)
            pool.wait_ge(scan_done, 1)
            pool.dma_start(g2_row, t["g2"]).then_inc(g2_in, 16)
            pool.dma_start(t["o_ssm_p"], small[:, 432:464]).then_inc(state_out, 16)
            pool.wait_ge(cv_ready, 1)
            pool.dma_start(t["o_conv_p"], cv_p[:, :, NP_TOK:NP_TOK + 2]).then_inc(state_out, 16)
            pool.dma_start(t["o_conv_s"], cv_s[:, :, :, NS:NS + 2]).then_inc(state_out, 16)
            for c in range(4, 12):
                v, h = (c - 4) // 2, c % 2
                pool.wait_ge(mod_row_ready, c + 1)
                pool.dma_start(mod_d[:, v, 512 * h:512 * h + 512], mod_out[:, h, :]).then_inc(mod_stored[h], 16)
            for h in range(2):
                pool.wait_ge(mod_stored[h], 64)
            rows = mod_d.rearrange("r v n -> r (v n)")
            flat = gates.rearrange("p v n -> p (v n)")
            flat_s = gates_s.rearrange("p v n -> p (v n)")
            pool.dma_start(flat, rows[0:1, :].partition_broadcast(P)).then_inc(gates_in, 16)
            for b in range(NB):
                pool.dma_start(flat_s[NS * b:NS * (b + 1), :],
                               rows[1 + b:2 + b, :].partition_broadcast(NS)).then_inc(gates_in, 16)
            pool.wait_ge(states_ready, 1)
            pool.dma_start(t["o_ssm_s"], st_s.rearrange("p r j b -> p (r j b)")).then_inc(state_out, 16)
            pool.wait_ge(yT_ready, FT)
            for i, (t0, n) in enumerate(TILES):
                src = t["x_prompt"][t0:t0 + n, :] if i < 4 else t["x_sample"]
                pool.dma_start(x1[0:n, i, :], src).then_inc(x_again, 16)
            pool.dma_start(fg, t["final_g"]).then_inc(x_again, 16)
            pool.dma_start(wr, t["w_router"]).then_inc(wr_in, 16)
            pool.dma_start(br, t["b_router"]).then_inc(wr_in, 16)
            pool.wait_ge(msm_ready, 1)
            pool.tensor_tensor(rstd_m, ms_m, half, ALU.pow).then_inc(mrstd_ready, 1)
            link(pool.memset(tri, 1.0))
            link(pool.affine_select(out=tri, in_=tri, compare_op=ALU.is_gt, fill=0.0, base=0,
                                    pattern=[[1, P]], channel_multiplier=-1))
            link(pool.memset(ones_b, 1.0))
            for out, pattern, base, mult in ((iota, [[1, P]], 0, 0), (w32, [[-1, NE]], NE, 0),
                                             (w4, [[-1, NG]], NG, 0), (tok_id, [[P, 5]], 0, 1),
                                             (full_at, [[CAP, RANKS - 1]], CAP, 0)):
                link(pool.iota(out, pattern=pattern, base=base, channel_multiplier=mult,
                               allow_small_or_imprecise_dtypes=True))
            pool.sem_inc(moe_consts, 1)
            for i, (t0, n) in enumerate(TILES):
                pool.wait_ge(ss_x1, i + 1)
                power(rstd[0:n, i:i + 1], ms[0:n, i:i + 1], ms[0:n, i:i + 1], D, rstd1_ready)
                pool.wait_ge(h2_ready, i + 1)
                pool.dma_start(h2_d[t0:t0 + n, :], h2[i % 2][0:n, :]).then_inc(h2_stored[i % 2], 16)
            wait_full(pool, job("rl", 4))
            for b in range(2):
                link(pool.memset(xg[b], 0.0))
            pool.wait_ge(h2_stored[0], 16 * 3)
            pool.wait_ge(h2_stored[1], 16 * 2)
            pool.wait_ge(route_ready, 1)
            passes = pool.value_load(npass[0:1, 0:1], min_val=1, max_val=RANKS)

            def gather(p, g, c):
                pool.wait_ge(idx_ready, count(p, g, c + 1))
                if g is not None or c >= 2:
                    pool.wait_ge(tr_done, count(p, g, c - 1))
                pool.sem_inc(rows_go, 1)
                pool.indirect_dma_start(
                    out=xg[c % 2], out_offset=None, in_=h2_d[:, :],
                    in_offset=bass.IndirectOffsetOnAxis(ap=idx[:, c % BODY, 1:2], axis=0),
                    bounds_check=TOK - 1, oob_is_err=False).then_inc(gathered[c % 2], 16)

            def scatter(p, g, c):
                pool.wait_ge(yo_ready, count(p, g, c + 1))
                pool.sem_inc(rows_go, 1)
                pool.indirect_dma_start(
                    out=y_d[:, :], in_=yo[c % 2], in_offset=None,
                    out_offset=bass.IndirectOffsetOnAxis(ap=idx[:, c % BODY, 0:1], axis=0),
                    bounds_check=2 * TOK - 1, oob_is_err=False).then_inc(scattered[c % 2], 16)

            def step(p, g, c):
                if g is not None or c + 3 < NE:
                    gather(p, g, c + 3)
                if g is not None or c >= 1:
                    scatter(p, g, c - 1)

            with pool.Fori(0, passes) as p:
                for c in range(3):
                    gather(p, None, c)
                for c in range(HEAD):
                    step(p, None, c)
                with pool.Fori(0, SPAN) as g:
                    for c in range(HEAD, HEAD + BODY):
                        step(p, g, c)
                for c in range(HEAD + BODY * SPAN, NE + 1):
                    step(p, None, c)
            for i, (t0, n) in enumerate(TILES):
                pool.wait_ge(ss_x2, i + 1)
                power(rstd[0:n, i:i + 1], ms[0:n, i:i + 1], ms[0:n, i:i + 1], D, rstd2_ready)
            pool.wait_ge(state_out, 16 * 4)

        @block.scalar
        def _(act):
            def link(ins):
                link.n += 1
                ins.then_inc(achain, 1)
                act.wait_ge(achain, link.n)
            link.n = 0

            def done(ins):
                ins.then_inc(bank_free["a"], 1)

            act.wait_ge(c_loaded, 16)
            nc.scalar.activation(silT, cT, ACT.Exp, scale=-1.0).then_inc(silu_e, 1)
            act.wait_ge(ang_ready, 1)
            nc.scalar.activation(sin_a, ang, ACT.Sin).then_inc(sin_ready, 1)
            nc.scalar.activation(sin_h, ang, ACT.Sin, scale=0.5).then_inc(sin_ready, 1)
            act.wait_ge(small_set, 1)
            for i, (t0, n) in enumerate(TILES):
                act.wait_ge(x_in[i], 16)
                if i > 0:
                    act.wait_ge(ss_x, i)
                nc.scalar.activation(junk_x[0:n, :], x_tok[0:n, i, :], ACT.Square,
                                     accum_out=ms[0:n, i:i + 1]).then_inc(ss_x, 1)
            wait_emptied(act, job("modT"))
            act.wait_ge(ss_x, 5)
            for i in range(4):
                n = job("xT", (i, 0))
                wait_full(act, n)
                for k in range(4):
                    ins = nc.scalar.activation(hT[:, k, P * i:P * (i + 1)], bank(n)[:, P * k:P * (k + 1)],
                                               ACT.Identity, bias=modT[:, k, 0:1], scale=modT[:, KT + k, 0:1])
                done(ins)
            act.wait_ge(consts, 3)
            for f in range(FT):
                n = job("zu", f)
                wait_full(act, n)
                done(nc.scalar.activation(u_ph[:, f, :, NB:YC],
                                          bank(n)[:, :].rearrange("p (c l) -> p l c", l=CH), ACT.Copy))
            n = job("zus")
            wait_full(act, n)
            src = bank(n)[:, 0:FT * NS_TOK].rearrange("p (f b s) -> p f s b", f=FT, b=NB)
            for f in range(FT):
                nc.scalar.activation(u_ph[:, f, 0:NS, 0:NB], src[:, f], ACT.Copy)
                ins = nc.scalar.activation(u_ph[:, f, CH - NS:CH, YC:UC], src[:, f], ACT.Copy)
            done(ins)
            for r in range(2):
                for q in range(4):
                    n = job("WT", (r, q))
                    wait_full(act, n)
                    done(nc.scalar.activation(WT[r][:, 4 * q:4 * q + 4, :].rearrange("p j n -> p (j n)"),
                                              bank(n)[:, :], ACT.Copy))
            for f in range(FT):
                for h in range(2):
                    n = job("U1", (f, h))
                    wait_full(act, n)
                    done(nc.scalar.activation(u_cm[:, 8 * f:8 * f + 8, 4 * h:4 * h + 4, :],
                                              bank(n)[0:UC, :].rearrange("p (l g h) -> p g l h", l=4, g=8), ACT.Copy))
            wait_emptied(act, job("xTs"))
            for q in range(4):
                for e in range(2):
                    n = job("G", (e, q))
                    wait_full(act, n)
                    done(nc.scalar.activation(g_sb[:, 8 * q + e:8 * q + 8:2, :],
                                              bank(n)[0:GH, :].rearrange("p (j n) -> p j n", j=4), ACT.Copy))
            for q in range(0, 8, 2):
                n = job("U2", q)
                wait_full(act, n)
                done(nc.scalar.activation(u_pk[:, 4 * q:4 * q + 4, :],
                                          bank(n)[:, 0:4 * UC].rearrange("p (g c) -> p g c", g=4), ACT.Copy))
            act.wait_ge(T_built, 16 * CH)
            for f in range(FT):
                n = job("zc", f)
                wait_full(act, n)
                done(nc.scalar.activation(y_conv[:, f, 0:NP_TOK], bank(n)[:, :], ACT.Copy))
            n = job("zcs")
            wait_full(act, n)
            done(nc.scalar.activation(y_conv[:, :, NP_TOK:TOK],
                                      bank(n)[:, 0:FT * NS_TOK].rearrange("p (f n) -> p f n", f=FT), ACT.Copy))
            act.wait_ge(conv_done, 1)
            act.wait_ge(state_out, 16 * 3)
            nc.scalar.activation(sqc, y_conv, ACT.Square).then_inc(sqc_ready, 1)
            for h in range(2):
                act.wait_ge(mod_stored[h], 64)
            for q in range(4):
                for e in range(2):
                    n = job("Y", (q, e))
                    wait_full(act, n)
                    done(nc.scalar.activation(y_cm[:, :, 8 * q + e:8 * q + 8:2, :].rearrange("p l g h -> p g l h"),
                                              bank(n)[0:YC, :].rearrange("p (g l h) -> p g l h", g=4, l=CH), ACT.Copy))
            for f in range(FT):
                act.wait_ge(yT_ready, f + 1)
                nc.scalar.activation(yT[:, f, :], yT[:, f, :], ACT.Gelu_apprx_tanh).then_inc(gelu_done, 1)
            for m in range(FT):
                n = job("gl", m)
                wait_full(act, n)
                done(nc.scalar.activation(sg[:, m, 0:NP_TOK], bank(n)[:, :], ACT.Sigmoid, bias=fvec[:, m, 1:2]))
            n = job("gls")
            wait_full(act, n)
            for m in range(FT):
                ins = nc.scalar.activation(sg[:, m, NP_TOK:TOK], bank(n)[:, NS_TOK * m:NS_TOK * (m + 1)],
                                           ACT.Sigmoid, bias=fvec[:, m, 1:2])
            done(ins)
            act.wait_ge(ysm_ready, 1)
            nc.scalar.activation(sq, sg, ACT.Square).then_inc(sq_ready, 1)

            act.wait_ge(mrstd_ready, 1)
            def conv_half(i, h):
                rows = TILES[i][1]
                n, q = job("mc", (i, h)), 2 * i + h
                wait_full(act, n)
                if q >= 4:
                    act.wait_ge(x1_ready, q - 3)
                done(nc.scalar.activation(mix_t[q % 4][0:rows, :], bank(n)[0:rows, :], ACT.Copy,
                                          scale=rstd_m[0:rows, i:i + 1]))

            for i, h in ((0, 0), (0, 1), (1, 0)):
                conv_half(i, h)
            for i in range(6):
                if i > 0:
                    rows = TILES[i - 1][1]
                    if i > 2:
                        wait_full(act, job("rl", i - 3))
                    for h in range(2):
                        n = job("hT", (i - 1, h))
                        wait_full(act, n)
                        done(nc.scalar.activation(h2T[(i - 1) % 2][:, 4 * h:4 * h + 4, 0:rows],
                                                  bank(n)[:, :].rearrange("p (k n) -> p k n", k=4)[:, :, 0:rows], ACT.Copy))
                if i < 4:
                    conv_half(i + 1, 1)
                if i < 5:
                    rows = TILES[i][1]
                    act.wait_ge(x1_ready, 2 * i + 2)
                    if i > 0:
                        act.wait_ge(rstd1_ready, i)
                    nc.scalar.activation(junk_m[0:rows, :], x1[0:rows, i, :], ACT.Square,
                                         accum_out=ms[0:rows, i:i + 1]).then_inc(ss_x1, 1)
                if i < 3:
                    conv_half(i + 2, 0)
            act.wait_ge(lg_ready, 1)
            nc.scalar.activation(ex, ex, ACT.Exp).then_inc(ex_ready, 1)
            act.wait_ge(d_ready, 1)
            nc.scalar.activation(wk[:, :, 0:1], wk[:, :, 0:1], ACT.Exp).then_inc(dex_ready, 1)

            act.wait_ge(route_ready, 1)
            passes = act.value_load(npass[0:1, 0:1], min_val=1, max_val=RANKS)

            def copy(out, src):
                return nc.scalar.activation(out, src, ACT.Copy)

            def hi_in(p, g, c):
                act.wait_ge(in_full[c % NSLOT], arrived(p, g, c))
                if g is not None or c >= 2:
                    act.wait_ge(gu_done, count(p, g, c - 1))
                for part in range(2):
                    copy(hi[c % 2][part], raw[c % NSLOT][part]).then_inc(hi_in_ready, 1)

            def hi_down(p, g, c):
                act.wait_ge(down_full[c % NSLOT], arrived(p, g, c))
                if g is not None or c >= 2:
                    act.wait_ge(down_done, count(p, g, c - 1))
                for part in (2, 3):
                    copy(hi[c % 2][part], raw[c % NSLOT][part]).then_inc(hi_down_ready, 1)

            def x_hi(p, g, c):
                act.wait_ge(tr_done, count(p, g, c + 1))
                if g is not None or c >= 2:
                    act.wait_ge(gu_done, count(p, g, c - 1))
                copy(xh[c % 2], banks[c % 2][:, :]).then_inc(xh_ready, 1)

            def silu(p, g, c):
                act.wait_ge(gu_done, count(p, g, c + 1))
                if g is not None or c >= 2:
                    act.wait_ge(he_ready, count(p, g, c - 1))
                nc.scalar.activation(gate_s[c % 2], banks[2 + c % 2][0:CAP, 0:DE], ACT.Silu).then_inc(gs_ready, 1)

            def he_hi(p, g, c):
                act.wait_ge(heT_done, count(p, g, c + 1))
                if g is not None or c >= 1:
                    act.wait_ge(down_done, count(p, g, c))
                copy(heh, banks[4][:, 0:2 * CAP]).then_inc(heh_ready, 1)

            def y_out_of_psum(p, g, c):
                act.wait_ge(down_done, count(p, g, c + 1))
                if g is not None or c >= 2:
                    act.wait_ge(scattered[c % 2], count(p, g, c, per=2, each=16))
                copy(yo[c % 2][:, 0:512], banks[6][0:CAP, :])
                copy(yo[c % 2][:, 512:1024], banks[7][0:CAP, :]).then_inc(yo_ready, 1)

            def step(p, g, c):
                if g is not None or c + 1 < NE:
                    hi_in(p, g, c + 1)
                if g is not None or c >= 1:
                    he_hi(p, g, c - 1)
                if g is not None or c < NE:
                    hi_down(p, g, c)
                    silu(p, g, c)
                if g is not None or c >= 1:
                    y_out_of_psum(p, g, c - 1)
                if g is not None or c + 2 < NE:
                    x_hi(p, g, c + 2)

            with act.Fori(0, passes) as p:
                act.wait_ge(pass_open, p + 1)
                hi_in(p, None, 0)
                for c in range(2):
                    x_hi(p, None, c)
                for c in range(HEAD):
                    step(p, None, c)
                with act.Fori(0, SPAN) as g:
                    for c in range(HEAD, HEAD + BODY):
                        step(p, g, c)
                for c in range(HEAD + BODY * SPAN, NE + 1):
                    step(p, None, c)
            def first_choice(i):
                n = TILES[i][1]
                act.wait_ge(y_in[i % 2], 16 * (i // 2 + 1))
                if i >= 2:
                    act.wait_ge(acc_ready, i - 1)
                nc.scalar.activation(acc[i % 2][0:n, :], y01[i % 2][0:n, 0, :], ACT.Copy,
                                     scale=wk[0:n, i, 0:1]).then_inc(y1_ready, 1)

            first_choice(0)
            for i, (t0, n) in enumerate(TILES):
                if i < 4:
                    first_choice(i + 1)
                act.wait_ge(acc_ready, i + 1)
                if i > 0:
                    act.wait_ge(ss_x2, i)
                nc.scalar.activation(junk[0:n, :], x1[0:n, i, :], ACT.Square, accum_out=ms[0:n, i:i + 1]).then_inc(ss_x2, 1)

        @block.vector
        def _(dve):
            V = nc.vector

            def link(ins):
                link.n += 1
                ins.then_inc(dchain, 1)
                dve.wait_ge(dchain, link.n)
            link.n = 0

            def done(ins):
                done.n += 1
                ins.then_inc(bank_free["v"], 1)
                dve.wait_ge(bank_free["v"], done.n)
            done.n = 0

            def tt(out, a, b, op):
                link(V.tensor_tensor(out, a, b, op))

            def ts(out, a, s1, op0, s2=None, op1=None):
                if op1 is None:
                    link(V.tensor_scalar(out, a, s1, None, op0))
                else:
                    link(V.tensor_scalar(out, a, s1, s2, op0, op1))

            def stt(out, a, s, b, op0, op1):
                link(V.scalar_tensor_tensor(out=out, in0=a, scalar=s, in1=b, op0=op0, op1=op1))

            def cmul(o, a, b, tmp_, conj=False, neg_im=False):
                tt(o[0], a[0], b[0], ALU.mult)
                tt(tmp_, a[1], b[1], ALU.mult)
                tt(o[0], o[0], tmp_, ALU.add if conj else ALU.subtract)
                tt(o[1], a[0], b[1], ALU.mult)
                tt(tmp_, a[1], b[0], ALU.mult)
                if neg_im:
                    stt(o[1], o[1], -1.0, tmp_, ALU.mult, ALU.subtract)
                else:
                    tt(o[1], o[1], tmp_, ALU.subtract if conj else ALU.add)

            MAGIC = 1.5 * 2.0 ** 23

            def exp_exact(out, x, k, r, bits):
                ts(k, x, 1.0 / math.log(2.0), ALU.mult, MAGIC, ALU.add)
                ts(k, k, -MAGIC, ALU.add, -126.0, ALU.max)
                ts(k, k, 127.0, ALU.min)
                stt(r, k, -0.693359375, x, ALU.mult, ALU.add)
                stt(r, k, 2.12194440e-4, r, ALU.mult, ALU.add)
                ts(out, r, 1.0 / 5040.0, ALU.mult)
                for c in (720.0, 120.0, 24.0, 6.0, 2.0, 1.0):
                    stt(out, out, 1.0 / c, r, ALU.add, ALU.mult)
                ts(bits, k, 127.0, ALU.add, 2.0 ** 23, ALU.mult)
                stt(out, out, 1.0, bits.bitcast(F32), ALU.add, ALU.mult)

            dve.wait_ge(silu_e, 1)
            ts(silT, silT, 1.0, ALU.add)
            link(V.reciprocal(silT, silT))
            V.tensor_tensor(silT, silT, cT, ALU.mult).then_inc(sil_ready, 1)
            dve.wait_ge(par_in, 16 * 2)
            exp_exact(dt_, ldt, k_, r_, bits_)
            tt(x_, lr, dt_, ALU.mult)
            exp_exact(mag, x_, k_, r_, bits_)
            tt(x_, li, dt_, ALU.mult)
            ts(k_, x_, 1.0 / (2.0 * math.pi), ALU.mult, MAGIC, ALU.add)
            ts(k_, k_, -MAGIC, ALU.add)
            stt(ang, k_, -6.28125, x_, ALU.mult, ALU.add)
            stt(ang, k_, -0.0019353071795864769, ang, ALU.mult, ALU.add)
            V.tensor_scalar(ang, ang, 3.1415925, -3.1415925, ALU.min, ALU.max).then_inc(ang_ready, 1)
            dve.wait_ge(sin_ready, 2)
            tt(cos_a, sin_h, sin_h, ALU.mult)
            ts(cos_a, cos_a, -2.0, ALU.mult, 1.0, ALU.add)
            a = [pw[0][:, :, 1], pw[1][:, :, 1]]
            tt(a[0], mag, cos_a, ALU.mult)
            tt(a[1], mag, sin_a, ALU.mult)
            link(V.memset(pw[0][:, :, 0:1], 1.0))
            link(V.memset(pw[1][:, :, 0:1], 0.0))
            for have in (1, 2, 4):
                top = [bc3(pw[r][:, :, have], [P, NJ, have]) for r in range(2)]
                cmul([pw[r][:, :, have + 1:2 * have + 1] for r in range(2)], top,
                     [pw[r][:, :, 1:have + 1] for r in range(2)], tmp_at(NJ, have))
            for r in range(2):
                link(V.tensor_copy(a4[r], pw[r][:, :, 4]))
            tt(den, lr, lr, ALU.mult)
            tt(x_, li, li, ALU.mult)
            tt(den, den, x_, ALU.add)
            link(V.reciprocal(den, den))
            ts(am1, a[0], -1.0, ALU.add)
            cmul([fr, fi], [lr, li], [am1, a[1]], x_, conj=True)
            tt(fr, fr, den, ALU.mult)
            tt(fi, fi, den, ALU.mult)
            cmul(bb, [bc3(fr, [P, NJ, GH]), bc3(fi, [P, NJ, GH])], b_in, tmp_at(NJ, GH))
            def w_position(l):
                cmul([w_p[r][:, :, l, :] for r in range(2)],
                     [bc3(pw[r][:, :, CH - 1 - l], [P, NJ, GH]) for r in range(2)], bb, tmp_at(NJ, GH))

            def ada_rows(c):
                n = job("ada", c)
                wait_full(dve, n)
                if c >= 4:
                    dve.wait_ge(bias_in[c % NBUF], 16 * ((c - 4) // NBUF + 1))
                bias = first_bias[:, 512 * c:512 * c + 512] if c < 4 else ada_bias[:, c % NBUF, :]
                h = c % 2
                if c < 4:
                    out = mod_row[:, 512 * c:512 * c + 512]
                else:
                    out = mod_out[:, h, :]
                    if c >= 6:
                        dve.wait_ge(mod_stored[h], 16 * ((c - 4) // 2))
                done(V.tensor_tensor(out, bank(n)[0:ROWS, :], bias, ALU.add))
                if c in (2, 3):
                    stt(out, out, 1.0, g1_row[:, 512 * h:512 * h + 512], ALU.add, ALU.mult)
                if c in (8, 9):
                    dve.wait_ge(g2_in, 16)
                    stt(out, out, 1.0, g2_row[:, 512 * h:512 * h + 512], ALU.add, ALU.mult)
                dve.sem_inc(mod_row_ready, 1)

            dve.sem_inc(bbar_ready, 1)
            dve.wait_ge(row_in, 16 * 3)
            for l in range(4):
                ada_rows(l)
                if l < 3:
                    w_position(l)
                if l == 1:
                    dve.wait_ge(rstd_ready, 1)
                    for i, (t0, n) in enumerate(TILES):
                        V.tensor_scalar(x_tok[0:n, i, :], x_tok[0:n, i, :], rstd[0:n, i:i + 1], None,
                                        ALU.mult).then_inc(xn_ready, 1)
            n = job("modT")
            wait_full(dve, n)
            done(V.tensor_copy(modT, bank(n)[:, 0:2 * KT * ROWS].rearrange("p (m r) -> p m r", r=ROWS)))
            for i in range(4):
                n = job("xT", (i, 1))
                wait_full(dve, n)
                for k in range(4, KT):
                    ins = V.tensor_scalar(hT[:, k, P * i:P * (i + 1)], bank(n)[:, P * (k - 4):P * (k - 3)],
                                          modT[:, KT + k, 0:1], modT[:, k, 0:1], ALU.mult, ALU.add)
                    if k < KT - 1:
                        link(ins)
                done(ins)
            n = job("xTs")
            wait_full(dve, n)
            hs = hT[:, :, NP_TOK:TOK].rearrange("p k (b s) -> p k b s", s=NS)
            ps = bank(n)[:, 0:KT * NS_TOK].rearrange("p (k b s) -> p k b s", k=KT, b=NB)
            for k in range(KT):
                sc_ = modT[:, KT + k, 1:ROWS].unsqueeze(2).to_broadcast([P, NB, NS])
                ins = V.tensor_tensor(hs[:, k], ps[:, k], sc_, ALU.mult)
                if k < KT - 1:
                    link(ins)
            done(ins)
            for k in range(KT):
                sh_ = modT[:, k, 1:ROWS].unsqueeze(2).to_broadcast([P, NB, NS])
                tt(hs[:, k], hs[:, k], sh_, ALU.add)
            dve.sem_inc(hs_ready, 1)
            w_position(3)
            dve.sem_inc(w_ready, 1)

            for d in range(6):
                cmul([CA[r][:, :, d, :] for r in range(2)],
                     [bc3(pw[r][:, :, d], [P, NJ, GH]) for r in range(2)], c_in, tmp_at(NJ, GH), neg_im=True)
            dve.sem_inc(ca_ready, 1)
            for q in range(1, 8, 2):
                n = job("U2", q)
                wait_full(dve, n)
                done(V.tensor_copy(u_pk[:, 4 * q:4 * q + 4, :], bank(n)[:, 0:4 * UC].rearrange("p (g c) -> p g c", g=4)))
            for q in range(4):
                for r in range(2):
                    n = job("S", (r, q))
                    wait_full(dve, n)
                    done(V.tensor_copy(S[r][:, 4 * q:4 * q + 4, :], bank(n)[:, 0:4 * UC].rearrange("p (j c) -> p j c", j=4)))
            cur = [cos_a, sin_a]
            for o in (ph[0], ph[1], ph[0]):
                cmul(o, cur, cur, x_)
                cur = o
            link(V.memset(E[0][:, :, 0:1], 1.0))
            link(V.memset(E[1][:, :, 0:1], 0.0))
            have = 1
            while have < NC:
                cmul([E[r][:, :, have:2 * have] for r in range(2)],
                     [bc3(cur[r], [P, NJ, have]) for r in range(2)],
                     [E[r][:, :, 0:have] for r in range(2)], rot_w[1][:, :, 0:have])
                nxt = ph[1] if cur is ph[0] else ph[0]
                cmul(nxt, cur, cur, x_)
                cur = nxt
                have *= 2
            tt(r8, mag, mag, ALU.mult)
            tt(r8, r8, r8, ALU.mult)
            tt(r8, r8, r8, ALU.mult)
            Sp = [S[r][:, :, NB:YC] for r in range(2)]
            cmul(rot_w, E, Sp, rot_a, conj=True)
            link(V.tensor_copy(rot_a, bc3(r8, [P, NJ, NC])))
            link(V.memset(rot_a[:, :, 0:1], 0.0))
            for r in range(2):
                flat = rot_w[r].rearrange("p j c -> p (j c)")
                link(V.tensor_tensor_scan(flat, rot_a.rearrange("p j c -> p (j c)"), flat, 0.0, ALU.mult, ALU.add))
            dve.wait_ge(h0_in, 32)
            cmul([X[r][:, :, NB + 1:] for r in range(2)], E, rot_w, rot_b)
            for r in range(2):
                link(V.memset(X[r][:, :, NB:NB + 1], 0.0))
            for r in range(2):
                link(V.tensor_copy(st_p[:, r], X[r][:, :, NB + NC]))
            dve.sem_inc(scan_done, 1)

            dve.wait_ge(T_built, 16 * CH)
            link(V.memset(cv_p[:, :, 0:2], 0.0))
            wait_emptied(dve, job("zcs"))
            for f in range(FT):
                n = job("zv", f)
                wait_full(dve, n)
                done(V.tensor_tensor(cv_p[:, f, 2:], bank(n)[:, :], y_conv[:, f, 0:NP_TOK], ALU.mult))
            n = job("zvs")
            wait_full(dve, n)
            samples = y_conv[:, :, NP_TOK:TOK].rearrange("p f (b s) -> p f b s", s=NS)
            for f in range(FT):
                ins = V.tensor_tensor(cv_s[:, f, :, 2:], bank(n)[:, NS_TOK * f:NS_TOK * (f + 1)].rearrange("p (b s) -> p b s", s=NS),
                                      samples[:, f], ALU.mult)
                if f < FT - 1:
                    link(ins)
            done(ins)
            dve.wait_ge(conv_in, 16)
            dve.sem_inc(cv_ready, 1)
            for f in range(FT):
                for out, src in ((y_conv[:, f, 0:NP_TOK], lambda k: cv_p[:, f, k:k + NP_TOK]),
                                 (samples[:, f], lambda k: cv_s[:, f, :, k:k + NS])):
                    ts(out, src(0), fvec[:, f, 4:5], ALU.mult)
                    for k in (1, 2):
                        stt(out, src(k), fvec[:, f, 4 + k:5 + k], out, ALU.mult, ALU.add)
            for f in range(FT):
                n = job("zb", f)
                wait_full(dve, n)
                done(V.tensor_tensor(y_conv[:, f, 0:NP_TOK], bank(n)[:, :], y_conv[:, f, 0:NP_TOK], ALU.mult))
            n = job("zbs")
            wait_full(dve, n)
            done(V.tensor_tensor(y_conv[:, :, NP_TOK:TOK], bank(n)[:, 0:FT * NS_TOK].rearrange("p (f n) -> p f n", f=FT),
                                 y_conv[:, :, NP_TOK:TOK], ALU.mult))
            dve.sem_inc(conv_done, 1)
            for c in range(4, 12):
                ada_rows(c)
            a4b = [bc3(a4[r], [P, NJ, NB]) for r in range(2)]
            cmul([st_s[:, r] for r in range(2)], a4b, [X[r][:, :, 0:NB] for r in range(2)], st_tmp)
            for r in range(2):
                tt(st_s[:, r], st_s[:, r], S[r][:, :, YC:UC], ALU.add)
            dve.sem_inc(states_ready, 1)

            for f in range(FT):
                for h in range(2):
                    n = job("YT", (f, h))
                    wait_full(dve, n)
                    pv = bank(n)[:, 0:4 * YC].rearrange("p (l c) -> p l c", l=4)
                    ls = slice(4 * h, 4 * h + 4)
                    if h == 0:
                        link(V.scalar_tensor_tensor(
                            out=yT[:, f, NP_TOK:TOK].rearrange("p (b s) -> p s b", s=NS), in0=u_ph[:, f, 0:NS, 0:NB],
                            scalar=fvec[:, f, 0:1], in1=pv[:, :, 0:NB], op0=ALU.mult, op1=ALU.add))
                    done(V.scalar_tensor_tensor(
                        out=yT[:, f, 0:NP_TOK].rearrange("p (c l) -> p l c", l=CH)[:, ls], in0=u_ph[:, f, ls, NB:YC],
                        scalar=fvec[:, f, 0:1], in1=pv[:, :, NB:YC], op0=ALU.mult, op1=ALU.add))
                dve.sem_inc(yT_ready, 1)
            def mean_squares(which):
                n = job("ss", which)
                wait_full(dve, n)
                c0 = 5 * which
                ts(ms_m[:, c0:c0 + 4], bank(n)[:, 0:4], 1.0 / (FT * P), ALU.mult, EPS, ALU.add)
                done(V.tensor_scalar(ms_m[0:NS_TOK, c0 + 4:c0 + 5], bank(n)[0:NS_TOK, 4:5], 1.0 / (FT * P), EPS,
                                     ALU.mult, ALU.add))

            mean_squares(0)
            for f in range(FT):
                ts(y_conv[:, f, :], y_conv[:, f, :], fvec[:, f, 2:3], ALU.mult)
            dve.sem_inc(yconv_ready, 1)
            wait_emptied(dve, job("gls"))
            tt(sg, sg, yT, ALU.mult)
            dve.sem_inc(ysm_ready, 1)
            dve.wait_ge(sq_ready, 1)
            for f in range(FT):
                ts(sg[:, f, :], sg[:, f, :], fvec[:, f, 3:4], ALU.mult)
            dve.sem_inc(ymix_ready, 1)
            mean_squares(1)
            dve.sem_inc(msm_ready, 1)

            dve.wait_ge(mrstd_ready, 1)
            dve.wait_ge(gates_in, 16 * (1 + NB))
            dve.wait_ge(x_again, 16 * 6)
            link(V.memset(logit, 0.0))
            dve.wait_ge(moe_consts, 1)
            link(V.tensor_scalar(vti[:, :, 0], tok_id, 2, None, ALU.arith_shift_right))
            link(V.tensor_scalar(vti[:, :, 1], tok_id, 3, None, ALU.bitwise_and))
            ts(vt[:, :, 1], vti[:, :, 1], 2.0, ALU.mult, 1.0, ALU.add)
            link(V.tensor_copy(vt[:, :, 0], vti[:, :, 0]))
            dve.wait_ge(wr_in, 32)
            for i in range(6):
                if i < 5:
                    rows = TILES[i][1]
                    gt = gates if i < 4 else gates_s
                    for h in range(2):
                        n = job("ms", (i, h))
                        wait_full(dve, n)
                        wait_emptied(dve, job("mc", (i, h)))
                        cols = slice(512 * h, 512 * h + 512)
                        m = mix_t[(2 * i + h) % 4][0:rows, :]
                        done(V.scalar_tensor_tensor(out=m, in0=bank(n)[0:rows, :], scalar=rstd_m[0:rows, 5 + i:6 + i],
                                                    in1=m, op0=ALU.mult, op1=ALU.add))
                        tt(m, m, gt[0:rows, 0, cols], ALU.mult)
                        V.tensor_tensor(x1[0:rows, i, cols], x1[0:rows, i, cols], m, ALU.add).then_inc(x1_ready, 1)
                    if i >= 2:
                        dve.wait_ge(h2_stored[i % 2], 16 * (i // 2))
                        wait_full(dve, job("hT", (i - 2, 1)))
                    else:
                        wait_full(dve, job("ss", 1))
                    dve.wait_ge(rstd1_ready, i + 1)
                    hv = h2[i % 2][0:rows, :]
                    stt(hv, x1[0:rows, i, :], rstd[0:rows, i:i + 1], gt[0:rows, 2, :], ALU.mult, ALU.mult)
                    V.tensor_tensor(hv, hv, gt[0:rows, 1, :], ALU.add).then_inc(h2_ready, 1)
                if i > 0:
                    n = job("rl", i - 1)
                    rows = TILES[i - 1][1]
                    wait_full(dve, n)
                    done(V.tensor_tensor(logit[0:rows, i - 1, :], bank(n)[0:rows, 0:NG + NE], br[0:rows, :], ALU.add))

            col = lambda c: gm[:, :, c:c + 1]
            wide = lambda c, w: col(c).to_broadcast([P, 5, w])
            lg, le = logit[:, :, 0:NG], logit[:, :, NG:NG + NE]
            link(V.tensor_reduce(col(0), lg, AX_X, ALU.max))
            V.tensor_tensor(ex, lg, wide(0, NG), ALU.subtract).then_inc(lg_ready, 1)

            def first_of(out, vals, top, weights, tie, w):
                tt(out, vals, wide(top, w), ALU.is_equal)
                tt(out, out, weights.unsqueeze(1).to_broadcast([P, 5, w]), ALU.mult)
                link(V.tensor_reduce(col(tie), out, AX_X, ALU.max))
                tt(out, out, wide(tie, w), ALU.is_equal)

            first_of(gone, lg, 0, w4, 1, NG)
            ts(gone, gone, BIG, ALU.mult, -BIG, ALU.add)
            tt(les.rearrange("p i (g e) -> p i g e", g=NG), le.rearrange("p i (g e) -> p i g e", g=NG),
               gone.unsqueeze(3).to_broadcast([P, 5, NG, NE_G]), ALU.add)
            link(V.tensor_reduce(col(2), les, AX_X, ALU.max))
            first_of(m1, les, 2, w32, 3, NE)
            stt(les, m1, -BIG, les, ALU.mult, ALU.add)
            link(V.tensor_reduce(col(4), les, AX_X, ALU.max))
            first_of(m2, les, 4, w32, 5, NE)
            V.tensor_tensor(wk[:, :, 0:1], col(4), col(2), ALU.subtract).then_inc(d_ready, 1)
            tt(mask, m1, m2, ALU.add)
            link(V.memset(mask[32:64, 4, :], 0.0))
            link(V.memset(mask[64:128, 4, :], 0.0))
            V.tensor_copy(mask_b, mask).then_inc(mask_ready, 1)
            dve.wait_ge(ex_ready, 1)
            link(V.tensor_reduce(col(6), ex, AX_X, ALU.add))
            dve.wait_ge(dex_ready, 1)
            ts(col(7), wk[:, :, 0:1], 1.0, ALU.add)
            tt(col(6), col(6), col(7), ALU.mult)
            link(V.reciprocal(col(6), col(6)))
            tt(wk[:, :, 1:2], wk[:, :, 0:1], col(6), ALU.mult)
            link(V.tensor_copy(wk[:, :, 0:1], col(6)))
            link(V.tensor_copy(vtok[:, :, :, 0], vt[:, :, 0:1].to_broadcast([P, 5, NE])))
            tt(vtok[:, :, :, 1], m2, vt[:, :, 1:2].to_broadcast([P, 5, NE]), ALU.add)
            n = job("pos")
            wait_full(dve, n)
            link(V.tensor_reduce(cnt[:, 0:1], bank(n)[:, 5 * NE:6 * NE], AX_X, ALU.max))
            done(V.scalar_tensor_tensor(out=posm, in0=bank(n)[:, 0:5 * NE].rearrange("p (i e) -> p i e", e=NE), scalar=1.0,
                                        in1=mask, op0=ALU.add, op1=ALU.mult))
            ts(posm, posm, -1.0, ALU.add)
            tt(more, cnt[:, 0:1].to_broadcast([P, RANKS - 1]), full_at, ALU.is_gt)
            link(V.tensor_reduce(cnt[:, 1:2], more, AX_X, ALU.add))
            ts(npass, cnt[:, 1:2], 1.0, ALU.add)
            dve.sem_inc(route_ready, 1)

            passes = dve.value_load(npass[0:1, 0:1], min_val=1, max_val=RANKS)

            def step_link(ins, s, value):
                ins.then_inc(s, 1)
                dve.wait_ge(s, value)

            def one_hot(p, g, c):
                if g is not None or c >= 2:
                    dve.wait_ge(idx_done, count(p, g, c - 1))
                k = number(g, c)
                src = posm[:, :, k:k + 1] if g is None else posm[:, :, bass.ds(k, 1)]
                V.tensor_tensor(onehot[c % 2], iota[:, 0:CAP].unsqueeze(1).to_broadcast([P, 5, CAP]),
                                src.to_broadcast([P, 5, CAP]), ALU.is_equal).then_inc(oh_ready, 1)

            def indices(p, g, c):
                dve.wait_ge(idx_done, count(p, g, c + 1))
                if g is not None or c >= BODY:
                    dve.wait_ge(scattered[c % 2], count(p, g, c - BODY + 2, per=2, each=16))
                at_ = lambda n: count(p, g, c, each=4) + n
                ps_ = banks[5][0:CAP, 0:2]
                row, token = idx[:, c % BODY, 0:1], idx[:, c % BODY, 1:2]
                step_link(V.tensor_scalar(idxf[:, 0:1], ps_[:, 0:1], 8.0, None, ALU.mult), idx_step, at_(1))
                step_link(V.tensor_tensor(idxf[:, 1:2], idxf[:, 0:1], ps_[:, 1:2], ALU.add), idx_step, at_(2))
                step_link(V.tensor_scalar(idxf[:, 2:3], idxf[:, 1:2], 0.0, OOB - 1.0, ALU.is_equal, ALU.mult), idx_step, at_(3))
                step_link(V.scalar_tensor_tensor(out=row, in0=idxf[:, 1:2], scalar=-1.0, in1=idxf[:, 2:3],
                                                 op0=ALU.add, op1=ALU.add), idx_step, at_(4))
                V.tensor_scalar(token, row, 1, None, ALU.arith_shift_right).then_inc(idx_ready, 1)

            def lo_in(p, g, c, part):
                dve.wait_ge(hi_in_ready, count(p, g, c, each=2) + part + 1)
                ins = V.tensor_tensor(lo[c % NSLOT][part], raw[c % NSLOT][part], hi[c % 2][part].bitcast(F32), ALU.subtract)
                if part == 1:
                    ins.then_inc(lo_in_ready, 1)

            def lo_down(p, g, c):
                for part in (2, 3):
                    dve.wait_ge(hi_down_ready, count(p, g, c, each=2) + part - 1)
                    ins = V.tensor_tensor(lo[c % NSLOT][part], raw[c % NSLOT][part], hi[c % 2][part].bitcast(F32), ALU.subtract)
                ins.then_inc(lo_down_ready, 1)

            def x_lo(p, g, c):
                dve.wait_ge(xh_ready, count(p, g, c + 1))
                V.tensor_tensor(xl[c % 2], banks[c % 2][:, :], xh[c % 2].bitcast(F32), ALU.subtract).then_inc(xl_ready, 1)

            def he_out(p, g, c):
                dve.wait_ge(gs_ready, count(p, g, c + 1))
                if g is not None or c >= 2:
                    dve.wait_ge(heT_done, count(p, g, c - 1))
                V.tensor_tensor(he[c % 2], gate_s[c % 2], banks[2 + c % 2][0:CAP, DE:2 * DE], ALU.mult).then_inc(he_ready, 1)

            def he_lo(p, g, c):
                dve.wait_ge(heh_ready, count(p, g, c + 1))
                V.tensor_tensor(hel, banks[4][:, 0:2 * CAP], heh.bitcast(F32), ALU.subtract).then_inc(hel_ready, 1)

            def step(p, g, c):
                if g is not None or c + 4 < NE:
                    one_hot(p, g, c + 4)
                if g is not None or c + 1 < NE:
                    lo_in(p, g, c + 1, 0)
                if g is not None or c >= 1:
                    he_lo(p, g, c - 1)
                if g is not None or c + 1 < NE:
                    lo_in(p, g, c + 1, 1)
                if g is not None or c < NE:
                    he_out(p, g, c)
                    lo_down(p, g, c)
                if g is not None or c + 2 < NE:
                    x_lo(p, g, c + 2)
                if g is not None or c + 4 < NE:
                    indices(p, g, c + 4)

            dve.sem_inc(pass_open, 1)
            with dve.Fori(0, passes) as p:
                for c in range(2):
                    one_hot(p, None, c)
                for c in range(2):
                    indices(p, None, c)
                one_hot(p, None, 2)
                indices(p, None, 2)
                one_hot(p, None, 3)
                lo_in(p, None, 0, 0)
                for c in range(2):
                    x_lo(p, None, c)
                indices(p, None, 3)
                lo_in(p, None, 0, 1)
                for c in range(HEAD):
                    step(p, None, c)
                with dve.Fori(0, SPAN) as g:
                    for c in range(HEAD, HEAD + BODY):
                        step(p, g, c)
                for c in range(HEAD + BODY * SPAN, NE + 1):
                    step(p, None, c)
                for b in range(2):
                    dve.wait_ge(scattered[b], p * (8 * NE) + 8 * NE)
                V.tensor_scalar(iota, iota, float(CAP), None, ALU.add).then_inc(pass_open, 1)
                dve.wait_ge(pass_open, p + 2)

            def add_up(i):
                rows = TILES[i][1]
                gt = (gates if i < 4 else gates_s)[0:rows, 3, :]
                dve.wait_ge(y1_ready, i + 1)
                a_ = acc[i % 2][0:rows, :]
                stt(a_, y01[i % 2][0:rows, 1, :], wk[0:rows, i, 1:2], a_, ALU.mult, ALU.add)
                tt(a_, a_, gt, ALU.mult)
                V.tensor_tensor(x1[0:rows, i, :], x1[0:rows, i, :], a_, ALU.add).then_inc(acc_ready, 1)

            def finish(i):
                rows = TILES[i][1]
                dve.wait_ge(rstd2_ready, i + 1)
                if i >= 2:
                    dve.wait_ge(y_out[i % 2], 16 * (i // 2))
                V.scalar_tensor_tensor(out=x2[i % 2][0:rows, :], in0=x1[0:rows, i, :], scalar=rstd[0:rows, i:i + 1],
                                       in1=fg[0:rows, :], op0=ALU.mult, op1=ALU.mult).then_inc(y_ready, 1)

            for i in range(6):
                if i < 5:
                    add_up(i)
                if i > 0:
                    finish(i - 1)

        @block.tensor
        def _(pe):
            mm = nc.tensor.matmul

            def fill(n, ins):
                ins.then_inc(bank_full, 1)

            def open_job(name, key=0):
                n = job(name, key)
                assert n == open_job.next
                open_job.next += 1
                if n >= 8:
                    wait_emptied(pe, n - 8)
                return n, bank(n)
            open_job.next = 0

            def block_at(kind, c=0):
                n = BLOCK_OF[(kind, c)]
                pe.wait_ge(block_in[n % NBUF], block_value(n))
                return block_buf[n % NBUF]

            def ada(c):
                w = block_at("ada", c)
                n, bk = open_job("ada", c)
                for k in range(KT):
                    ins = mm(bk[0:ROWS, :], silT[:, k, :], w[:, k, :], start=(k == 0), stop=(k == KT - 1))
                fill(n, ins)

            def open_samples(name):
                n = job(name)
                wait_emptied(pe, n - 8)
                return n, bank(n)

            def project(c, name):
                w = block_at("in", c)
                ns, bs = open_samples(name + "s")

                def samples_of(f, k):
                    return mm(bs[:, NS_TOK * f:NS_TOK * (f + 1)], w[:, k, P * f:P * (f + 1)], hT[:, k, NP_TOK:TOK],
                              start=(k == 0), stop=(k == KT - 1))

                for f in range(FT):
                    n, bk = open_job(name, f)
                    if f == 1:
                        pe.wait_ge(hs_ready, 1)
                    for k in range(KT):
                        if f > 0:
                            samples_of(f - 1, k)
                        ins = mm(bk[:, :], w[:, k, P * f:P * (f + 1)], hT[:, k, 0:NP_TOK], start=(k == 0), stop=(k == KT - 1))
                    fill(n, ins)
                assert open_job(name + "s")[0] == ns
                for k in range(KT):
                    ins = samples_of(FT - 1, k)
                fill(ns, ins)

            pe.wait_ge(sil_ready, 1)
            for c in range(4):
                ada(c)
            pe.wait_ge(consts, 1)
            pe.wait_ge(mod_row_ready, 4)
            n, bk = open_job("modT")
            for m in range(2 * KT):
                ins = nc.tensor.transpose(bk[:, ROWS * m:ROWS * (m + 1)], mod_row[:, P * m:P * (m + 1)], ident[0:ROWS, 0:ROWS])
            fill(n, ins)
            for i in range(4):
                pe.wait_ge(xn_ready, i + 1)
                for h in range(2):
                    n, bk = open_job("xT", (i, h))
                    for k in range(4):
                        ins = nc.tensor.transpose(bk[:, P * k:P * (k + 1)], x_tok[:, i, P * (4 * h + k):P * (4 * h + k + 1)], ident)
                    fill(n, ins)
            pe.wait_ge(xn_ready, 5)
            n, bk = open_job("xTs")
            for k in range(KT):
                ins = nc.tensor.transpose(bk[:, NS_TOK * k:NS_TOK * (k + 1)], x_tok[0:NS_TOK, 4, P * k:P * (k + 1)],
                                          ident[0:NS_TOK, 0:NS_TOK])
            fill(n, ins)
            wait_emptied(pe, job("xT", (3, 0)))
            wait_emptied(pe, job("xT", (3, 1)))
            project(0, "zu")
            pe.wait_ge(w_ready, 2)
            for r in range(2):
                for q in range(4):
                    n, bk = open_job("WT", (r, q))
                    for j in range(4):
                        ins = nc.tensor.transpose(bk[:, P * j:P * (j + 1)],
                                                  w_p[r][:, 4 * q + j].rearrange("p l h -> p (l h)"), ident)
                    fill(n, ins)
            wait_emptied(pe, job("zus"))
            for f in range(FT):
                for h in range(2):
                    n, bk = open_job("U1", (f, h))
                    for l in range(4):
                        ins = nc.tensor.transpose(bk[0:UC, P * l:P * (l + 1)], u_ph[:, f, 4 * h + l, :], ident)
                    fill(n, ins)
            pe.wait_ge(ca_ready, 2)
            for q in range(4):
                for e in range(2):
                    n, bk = open_job("G", (e, q))
                    half_p = slice(ST * e, ST * (e + 1))
                    for j in range(4):
                        for r in range(2):
                            ins = mm(bk[0:GH, P * j:P * (j + 1)], bb[r][half_p, 4 * q + j, :],
                                     CA[r][half_p, 4 * q + j, 0:CH, :].rearrange("p d h -> p (d h)"),
                                     start=(r == 0), stop=(r == 1))
                    fill(n, ins)
            wait_emptied(pe, job("U1", (3, 1)))
            for q in range(8):
                n, bk = open_job("U2", q)
                for g in range(4):
                    ins = nc.tensor.transpose(bk[:, UC * g:UC * (g + 1)], u_cm[:, 4 * q + g].rearrange("p l h -> p (l h)"),
                                              ident[0:UC, 0:UC])
                fill(n, ins)
            wait_emptied(pe, job("U2", 6))
            wait_emptied(pe, job("U2", 7))
            for q in range(4):
                for r in range(2):
                    n, bk = open_job("S", (r, q))
                    for j in range(4):
                        for e in range(2):
                            ins = mm(bk[ST * e:ST * (e + 1), UC * j:UC * (j + 1)], WT[r][:, 4 * q + j, ST * e:ST * (e + 1)],
                                     u_pk[:, 2 * (4 * q + j) + e, :], start=True, stop=True)
                    fill(n, ins)
            project(1, "zc")
            project(2, "zv")
            project(3, "zb")
            for c in range(4, 12):
                ada(c)
            pe.wait_ge(scan_done, 1)
            pe.wait_ge(T_built, 16 * CH)
            for q in range(4):
                for e in range(2):
                    n, bk = open_job("Y", (q, e))
                    half_p = slice(ST * e, ST * (e + 1))
                    for j in range(4):
                        jj = 4 * q + j
                        out = bk[0:YC, P * j:P * (j + 1)]
                        mm(out, u_pk[:, 2 * jj + e, 0:YC], T[:, 2 * jj + e, :], start=True, stop=False)
                        for r in range(2):
                            ins = mm(out, X[r][half_p, jj, 0:YC],
                                     CA[r][half_p, jj, 1:CH + 1, :].rearrange("p d h -> p (d h)"),
                                     start=False, stop=(r == 1))
                    fill(n, ins)
            wait_emptied(pe, job("Y", (3, 1)))
            for f in range(FT):
                for h in range(2):
                    n, bk = open_job("YT", (f, h))
                    for l in range(4):
                        ins = nc.tensor.transpose(bk[:, YC * l:YC * (l + 1)], y_cm[:, 4 * h + l, 8 * f:8 * f + 8, :].rearrange("p g h -> p (g h)"),
                                                  ident[0:YC, 0:YC])
                    fill(n, ins)

            def squares(which, src):
                n, bk = open_job("ss", which)
                pe.wait_ge(consts, 2)
                for i, (t0, rows) in enumerate(TILES):
                    for k in range(FT):
                        ins = mm(bk[0:rows, i:i + 1], src[:, k, t0:t0 + rows], one, start=(k == 0), stop=(k == FT - 1))
                fill(n, ins)

            pe.wait_ge(sqc_ready, 1)
            squares(0, sqc)
            w = block_at("glu")
            ns, bs = open_samples("gls")

            def samples_of(m, k):
                return mm(bs[:, NS_TOK * m:NS_TOK * (m + 1)], w[:, k, P * m:P * (m + 1)], yT[:, k, NP_TOK:TOK],
                          start=(k == 0), stop=(k == FT - 1))

            for m in range(FT):
                n, bk = open_job("gl", m)
                for k in range(FT):
                    pe.wait_ge(gelu_done, k + 1)
                    if m > 0:
                        samples_of(m - 1, k)
                    ins = mm(bk[:, :], w[:, k, P * m:P * (m + 1)], yT[:, k, 0:NP_TOK], start=(k == 0), stop=(k == FT - 1))
                fill(n, ins)
            assert open_job("gls")[0] == ns
            for k in range(FT):
                ins = samples_of(FT - 1, k)
            fill(ns, ins)

            def mixed(name, i, h):
                t0, rows = TILES[i]
                src, k0 = {"mc": (y_conv, 0), "ms": (sg, FT)}[name]
                n, bk = open_job(name, (i, h))
                for k in range(FT):
                    ins = mm(bk[0:rows, :], src[:, k, t0:t0 + rows], wo[h][:, k0 + k, :], start=(k == 0), stop=(k == FT - 1))
                fill(n, ins)

            pe.wait_ge(yconv_ready, 1)
            wo = [block_at("out", c) for c in range(2)]
            for i, h in ((0, 0), (0, 1), (1, 0)):
                mixed("mc", i, h)
            pe.wait_ge(sq_ready, 1)
            squares(1, sq)
            pe.wait_ge(ymix_ready, 1)
            for i in range(6):
                if i < 5:
                    mixed("ms", i, 0)
                if i > 0:
                    rows = TILES[i - 1][1]
                    pe.wait_ge(h2_ready, i)
                    for h in range(2):
                        n, bk = open_job("hT", (i - 1, h))
                        for k in range(4):
                            kk = 4 * h + k
                            ins = nc.tensor.transpose(bk[:, P * k:P * k + rows], h2[(i - 1) % 2][0:rows, P * kk:P * (kk + 1)],
                                                      ident[0:rows, 0:rows])
                        fill(n, ins)
                if i < 4:
                    mixed("mc", i + 1, 1)
                if i < 5:
                    mixed("ms", i, 1)
                if i < 3:
                    mixed("mc", i + 2, 0)
                if i > 0:
                    rows = TILES[i - 1][1]
                    n, bk = open_job("rl", i - 1)
                    wait_emptied(pe, job("hT", (i - 1, 1)))
                    pe.wait_ge(wr_in, 32)
                    for k in range(KT):
                        ins = mm(bk[0:rows, 0:NG + NE], h2T[(i - 1) % 2][:, k, 0:rows], wr[:, k, :],
                                 start=(k == 0), stop=(k == KT - 1))
                    fill(n, ins)
            pe.wait_ge(mask_ready, 1)
            n, bk = open_job("pos")
            for i in range(6):
                out = bk[:, NE * i:NE * (i + 1)]
                for j in range(min(i, 4) + 1):
                    own = j == i
                    ins = mm(out, tri if own else ones_b, mask_b[:, j, :], start=(j == 0), stop=(j == min(i, 4)))
            fill(n, ins)
            wait_emptied(pe, job("pos"))
            wait_emptied(pe, job("hT", (4, 1)))

            pe.wait_ge(route_ready, 1)
            passes = pe.value_load(npass[0:1, 0:1], min_val=1, max_val=RANKS)

            def find(p, g, c):
                pe.wait_ge(oh_ready, count(p, g, c + 1))
                if g is not None or c >= 1:
                    pe.wait_ge(idx_ready, count(p, g, c))
                k = number(g, c)
                for i in range(5):
                    v = vtok[:, i, k, :] if g is None else vtok[:, i, bass.ds(k, 1), :].rearrange("p o v -> p (o v)")
                    ins = mm(banks[5][0:CAP, 0:2], onehot[c % 2][:, i, :], v, start=(i == 0), stop=(i == 4))
                ins.then_inc(idx_done, 1)

            def turn(p, g, c):
                pe.wait_ge(gathered[c % 2], count(p, g, c + 2, per=2, each=16))
                if g is not None or c >= 2:
                    pe.wait_ge(xl_ready, count(p, g, c - 1))
                pe.sem_inc(turn_go, 1)
                for h in range(KT):
                    ins = nc.tensor.transpose(banks[c % 2][:, CAP * h:CAP * (h + 1)], xg[c % 2][:, P * h:P * (h + 1)],
                                              ident[0:CAP, 0:CAP])
                ins.then_inc(tr_done, 1)

            def gate_up(p, g, c, which):
                b, s = c % 2, c % NSLOT
                out = banks[2 + b][0:CAP, :]
                if which == "hi":
                    pe.wait_ge(xl_ready, count(p, g, c + 1))
                    pe.wait_ge(hi_in_ready, count(p, g, c + 1, each=2))
                    if g is not None or c >= 2:
                        pe.wait_ge(he_ready, count(p, g, c - 1))
                    terms = [(x, hi[b]) for x in (xh[b], xl[b])]
                else:
                    pe.wait_ge(lo_in_ready, count(p, g, c + 1))
                    terms = [(xh[b], lo[s])]
                for n, (x, w) in enumerate(terms):
                    for h in range(KT):
                        ins = mm(out, x[:, CAP * h:CAP * (h + 1)], w[h // 4][:, 512 * (h % 4):512 * (h % 4 + 1)],
                                 start=(which == "hi" and n == 0 and h == 0), stop=(which == "lo" and h == KT - 1))
                if which == "lo":
                    ins.then_inc(gu_done, 1)

            def turn_he(p, g, c):
                pe.wait_ge(he_ready, count(p, g, c + 1))
                if g is not None or c >= 1:
                    pe.wait_ge(hel_ready, count(p, g, c))
                pe.sem_inc(turn_go, 1)
                for h in range(2):
                    ins = nc.tensor.transpose(banks[4][:, CAP * h:CAP * (h + 1)], he[c % 2][:, P * h:P * (h + 1)],
                                              ident[0:CAP, 0:CAP])
                ins.then_inc(heT_done, 1)

            def down(p, g, c):
                b, s = c % 2, c % NSLOT
                pe.wait_ge(hel_ready, count(p, g, c + 1))
                pe.wait_ge(lo_down_ready, count(p, g, c + 1))
                if g is not None or c >= 1:
                    pe.wait_ge(yo_ready, count(p, g, c))
                for col in range(2):
                    for n, (x, w) in enumerate(((heh, hi[b]), (hel, hi[b]), (heh, lo[s]))):
                        for h in range(2):
                            ins = mm(banks[6 + col][0:CAP, :], x[:, CAP * h:CAP * (h + 1)], w[2 + h][:, 512 * col:512 * col + 512],
                                     start=(n == 0 and h == 0), stop=(n == 2 and h == 1))
                ins.then_inc(down_done, 1)

            def step(p, g, c):
                if g is not None or c < NE:
                    gate_up(p, g, c, "hi")
                if g is not None or c >= 1:
                    turn_he(p, g, c - 1)
                if g is not None or c < NE:
                    gate_up(p, g, c, "lo")
                if g is not None or c >= 1:
                    down(p, g, c - 1)
                if g is not None or c + 2 < NE:
                    turn(p, g, c + 2)
                if g is not None or c + 4 < NE:
                    find(p, g, c + 4)

            with pe.Fori(0, passes) as p:
                pe.wait_ge(pass_open, p + 1)
                for c in range(3):
                    find(p, None, c)
                for c in range(2):
                    turn(p, None, c)
                find(p, None, 3)
                for c in range(HEAD):
                    step(p, None, c)
                with pe.Fori(0, SPAN) as g:
                    for c in range(HEAD, HEAD + BODY):
                        step(p, g, c)
                for c in range(HEAD + BODY * SPAN, NE + 1):
                    step(p, None, c)


OUTS = {"y_prompt": (NP_TOK, D), "y_sample": (NS_TOK, D), "o_conv_p": (P, FT, 2), "o_conv_s": (P, FT, NB, 2),
        "o_ssm_p": (P, 2 * NJ), "o_ssm_s": (P, 2 * NJ * NB)}


def kernel(**inputs):
    import numpy as np
    import concourse.bacc as _bacc
    from concourse import mybir as _mybir
    from concourse.bass_utils import run_bass_kernel_spmd as _run

    x = {k: np.asarray(v) for k, v in inputs.items()}

    def states(a):
        a = a.reshape((NJ, 2, ST) + a.shape[2:])
        return np.moveaxis(a, 0, 2).reshape((P, NJ) + a.shape[3:])

    def feats(a):
        return np.moveaxis(a.reshape(a.shape[:-1] + (FT, P)), (-1, -2), (0, 1))

    def blocks(w, n):
        k = w.shape[0] // P
        return w.reshape(k, P, n, 512).transpose(2, 1, 0, 3).reshape(n, P, k * 512)

    w_in = x["w_in"][0].reshape(D, 4, 512)[:, [3, 1, 2, 0], :].reshape(D, 4 * 512)
    c = np.concatenate([x["c_prompt"], x["c_sample"]], 0)
    gate_up = np.concatenate([x["w_expert_gate"][0], x["w_expert_up"][0]], 2)
    gate_up = gate_up.reshape(NE, KT, P, 2 * DE).transpose(0, 2, 1, 3).reshape(NE, P, KT * 2 * DE)
    down = x["w_expert_down"][0].reshape(NE, 2, P, D).transpose(0, 2, 1, 3).reshape(NE, P, 2 * D)
    router = np.concatenate([x["w_router_group"][0], x["w_router_expert"][0].transpose(1, 0, 2).reshape(D, NE)], 1)
    b_router = np.concatenate([x["b_router_group"][0], x["b_router_expert"][0].reshape(NE)])
    vectors = [x["ssm_d"][0], x["b_glu"][0], x["out_norm_conv_g"][0], x["out_norm_ssm_g"][0], *x["conv_w"][0]]
    arrays = {
        "x_prompt": x["x_prompt"][0], "x_sample": x["x_sample"].reshape(NS_TOK, D),
        "cT": c.reshape(ROWS, KT, P).transpose(2, 1, 0),
        "w_ada": blocks(x["w_ada"][0], 12), "w_in": blocks(w_in, 4), "w_out": blocks(x["w_out"][0], 2),
        "w_glu": blocks(x["w_glu"][0], 1)[0], "w_exp": np.concatenate([gate_up, down], 2),
        "b_ada": np.broadcast_to(x["b_ada"][0], (ROWS, 6 * D)),
        "g1": np.broadcast_to(x["norm1_g"][0], (ROWS, D)), "g2": np.broadcast_to(x["norm2_g"][0], (ROWS, D)),
        "final_g": np.broadcast_to(x["final_norm_g"], (P, D)),
        "w_router": router.reshape(KT, P, NG + NE).transpose(1, 0, 2), "b_router": np.broadcast_to(b_router, (P, NG + NE)),
        "lam": np.stack([states(x["lambda_re"][0]), states(x["lambda_im"][0]),
                         states(np.broadcast_to(x["log_dt"][0][:, None], (GR, ST)))], 1),
        "bc": np.stack([states(x["ssm_b_re"][0]).reshape(P, -1), states(x["ssm_b_im"][0]).reshape(P, -1),
                        states(x["ssm_c_re"][0].transpose(0, 2, 1)).reshape(P, -1),
                        states(x["ssm_c_im"][0].transpose(0, 2, 1)).reshape(P, -1)], 1),
        "fvec": np.stack([feats(v) for v in vectors], 2),
        "conv_state": feats(x["state_conv"][0]),
        "h0": np.stack([states(x[k][0].transpose(1, 2, 0)) for k in ("state_ssm_re", "state_ssm_im")], 0),
    }
    arrays = {k: np.ascontiguousarray(v) for k, v in arrays.items()}
    nc = _bacc.Bacc("TRN2", target_bir_lowering=False, num_devices=1)
    t = {}
    for name, a in arrays.items():
        t[name] = nc.dram_tensor(f"in_{name}", a.shape, _mybir.dt.from_np(a.dtype), kind="ExternalInput").ap()
    for name, shape in OUTS.items():
        t[name] = nc.dram_tensor(f"out_{name}", shape, _mybir.dt.float32, kind="ExternalOutput").ap()
    build(nc, t)
    r = _run(nc, [{f"in_{k}": a for k, a in arrays.items()}], core_ids=[0]).results[0]
    o = {k: np.asarray(r[f"out_{k}"]) for k in OUTS}

    def groups(a):
        a = a.reshape((2, ST, NJ) + a.shape[2:])
        a = np.moveaxis(a, (2, 0, 1), (-3, -2, -1))
        return a.reshape(a.shape[:-3] + (GR, ST))

    conv_p = o["o_conv_p"].transpose(2, 1, 0).reshape(1, 1, 2, FT * P)
    conv_s = o["o_conv_s"].transpose(2, 3, 1, 0).reshape(1, NB, 2, FT * P)
    ssm_p = o["o_ssm_p"].reshape(P, 2, NJ)
    ssm_s = o["o_ssm_s"].reshape(P, 2, NJ, NB)
    return (o["y_prompt"].reshape(1, NP_TOK, D), o["y_sample"].reshape(NB, NS, D), conv_p,
            groups(ssm_p[:, 0]).reshape(1, 1, GR, ST), groups(ssm_p[:, 1]).reshape(1, 1, GR, ST),
            conv_s, groups(ssm_s[:, 0]).reshape(1, NB, GR, ST), groups(ssm_s[:, 1]).reshape(1, NB, GR, ST))
```
